# Optimizing a Trainium2 kernel written in Bass

```python
import jax, jax.numpy as jnp
from jax import lax
import numpy as np

D_MODEL = 1024
BATCH = 1
SEQ = 256
DEPTH = 2

FOURIER_GROUPS = 4
FOURIER_GROUP_DIM = D_MODEL // 8
FOURIER_WIDTH = FOURIER_GROUPS * FOURIER_GROUP_DIM
GMLP_GROUPS = 4
GMLP_GROUP_DIM = D_MODEL // 8
GMLP_WIDTH = GMLP_GROUPS * GMLP_GROUP_DIM
CHUNK = 128
N_BRANCH = 2
D_IN = FOURIER_WIDTH + 2 * GMLP_WIDTH + N_BRANCH * D_MODEL
D_FF_DENSE = 11 * D_MODEL // 4
N_EXPERTS = 8
TOP_K = 2
D_FF_EXPERT = 7 * D_MODEL // 2
N_DENSE = (DEPTH + 1) // 2
N_MOE = DEPTH // 2
RMS_EPS = 1e-6
LN_EPS = 1e-5

kernel_name = 'hybrid_fourier_gmlp_moe_encoder'

def rms_norm(x, g):
    xf = x.astype(jnp.float32)
    y = xf * lax.rsqrt(jnp.mean(xf * xf, axis=-1, keepdims=True) + RMS_EPS)
    return (y * g.astype(jnp.float32)).astype(x.dtype)

def layer_norm(x, g, b):
    xf = x.astype(jnp.float32)
    mu = jnp.mean(xf, axis=-1, keepdims=True)
    xc = xf - mu
    var = jnp.mean(xc * xc, axis=-1, keepdims=True)
    y = xc * lax.rsqrt(var + LN_EPS) * g.astype(jnp.float32) + b.astype(jnp.float32)
    return y.astype(x.dtype)

def fourier_mix(a):
    af = a.astype(jnp.float32)
    return jnp.fft.fft2(af, axes=(1, 3), norm='ortho').real.astype(a.dtype)

def spatial_gating(u, v, w_s, b_s, ln_g, ln_b):
    B, S, _ = v.shape
    v = layer_norm(v, ln_g, ln_b)
    v = v.reshape(B, S // CHUNK, CHUNK, GMLP_GROUPS, GMLP_GROUP_DIM)
    sv = jnp.einsum('gpq,bcqgd->bcpgd', w_s, v) + jnp.transpose(b_s)[:, :, None]
    return u * sv.reshape(B, S, GMLP_WIDTH)

def token_mixer(h, w_in, w_fourier, w_gmlp, w_out, w_s, b_s, ln_g, ln_b):
    B, S, D = h.shape
    z = jnp.einsum('bsd,de->bse', h, w_in)
    c1 = FOURIER_WIDTH
    c2 = c1 + GMLP_WIDTH
    c3 = c2 + GMLP_WIDTH
    za, zu, zv, zg = z[..., :c1], z[..., c1:c2], z[..., c2:c3], z[..., c3:]
    fa = fourier_mix(za.reshape(B, S, FOURIER_GROUPS, FOURIER_GROUP_DIM)).reshape(B, S, FOURIER_WIDTH)
    ya = jnp.einsum('bsf,fd->bsd', fa, w_fourier)
    sg = spatial_gating(jax.nn.gelu(zu, approximate=False), jax.nn.gelu(zv, approximate=False),
                        w_s, b_s, ln_g, ln_b)
    yb = jnp.einsum('bsf,fd->bsd', sg, w_gmlp)
    g = jax.nn.sigmoid(zg.reshape(B, S, N_BRANCH, D))
    m = g[:, :, 0, :] * ya + g[:, :, 1, :] * yb
    return jnp.einsum('bsd,de->bse', m, w_out)

def swiglu(h, w1, w3, w2):
    a = jnp.einsum('...d,df->...f', h, w1)
    b = jnp.einsum('...d,df->...f', h, w3)
    return jnp.einsum('...f,fd->...d', jax.nn.silu(a) * b, w2)

def moe_swiglu(h, router_w, router_b, w1, w3, w2):
    B, S, D = h.shape
    t = h.reshape(B * S, D)
    logits = jnp.einsum('td,de->te', t, router_w).astype(jnp.float32) + router_b.astype(jnp.float32)
    top_vals, top_idx = lax.top_k(logits, TOP_K)
    top_w = jax.nn.softmax(top_vals, axis=-1)
    gate = jnp.sum(jax.nn.one_hot(top_idx, N_EXPERTS, dtype=jnp.float32) * top_w[..., None], axis=1)
    gate = gate.astype(t.dtype)
    out = jnp.zeros_like(t)
    for e in range(N_EXPERTS):
        out = out + gate[:, e:e + 1] * swiglu(t, w1[e], w3[e], w2[e])
    return out.reshape(B, S, D)

def setup_inputs(seed: int = 0) -> dict:
    key = jax.random.key(seed)
    ks = jax.random.split(key, 24)
    f32 = jnp.float32
    nrm = lambda k, shape, fan_in: jax.random.normal(k, shape, f32) * (fan_in ** -0.5)
    gain = lambda k, shape: 1.0 + 0.02 * jax.random.normal(k, shape, f32)
    small = lambda k, shape, s: s * jax.random.normal(k, shape, f32)
    return {
        'x': jax.random.normal(ks[0], (BATCH, SEQ, D_MODEL), f32),
        'pre_mix_g': gain(ks[1], (DEPTH, D_MODEL)),
        'post_mix_g': gain(ks[2], (DEPTH, D_MODEL)),
        'w_in': nrm(ks[3], (DEPTH, D_MODEL, D_IN), D_MODEL),
        'w_fourier': nrm(ks[4], (DEPTH, FOURIER_WIDTH, D_MODEL), FOURIER_WIDTH),
        'w_gmlp': nrm(ks[5], (DEPTH, GMLP_WIDTH, D_MODEL), GMLP_WIDTH),
        'w_out': nrm(ks[6], (DEPTH, D_MODEL, D_MODEL), D_MODEL),
        'w_spatial': nrm(ks[7], (DEPTH, GMLP_GROUPS, CHUNK, CHUNK), CHUNK),
        'b_spatial': gain(ks[8], (DEPTH, GMLP_GROUPS, CHUNK)),
        'gmlp_ln_g': gain(ks[9], (DEPTH, GMLP_WIDTH)),
        'gmlp_ln_b': small(ks[10], (DEPTH, GMLP_WIDTH), 0.02),
        'pre_ffn_g': gain(ks[11], (DEPTH, D_MODEL)),
        'post_ffn_g': gain(ks[12], (DEPTH, D_MODEL)),
        'ffn_w1': nrm(ks[13], (N_DENSE, D_MODEL, D_FF_DENSE), D_MODEL),
        'ffn_w3': nrm(ks[14], (N_DENSE, D_MODEL, D_FF_DENSE), D_MODEL),
        'ffn_w2': nrm(ks[15], (N_DENSE, D_FF_DENSE, D_MODEL), D_FF_DENSE),
        'router_w': nrm(ks[16], (N_MOE, D_MODEL, N_EXPERTS), D_MODEL),
        'router_b': small(ks[17], (N_MOE, N_EXPERTS), 0.01),
        'moe_w1': nrm(ks[18], (N_MOE, N_EXPERTS, D_MODEL, D_FF_EXPERT), D_MODEL),
        'moe_w3': nrm(ks[19], (N_MOE, N_EXPERTS, D_MODEL, D_FF_EXPERT), D_MODEL),
        'moe_w2': nrm(ks[20], (N_MOE, N_EXPERTS, D_FF_EXPERT, D_MODEL), D_FF_EXPERT),
    }

def reference(x, pre_mix_g, post_mix_g, w_in, w_fourier, w_gmlp, w_out, w_spatial, b_spatial,
              gmlp_ln_g, gmlp_ln_b, pre_ffn_g, post_ffn_g, ffn_w1, ffn_w3, ffn_w2,
              router_w, router_b, moe_w1, moe_w3, moe_w2):
    for l in range(DEPTH):
        h = rms_norm(x, pre_mix_g[l])
        y = token_mixer(h, w_in[l], w_fourier[l], w_gmlp[l], w_out[l], w_spatial[l], b_spatial[l],
                        gmlp_ln_g[l], gmlp_ln_b[l])
        x = x + rms_norm(y, post_mix_g[l])
        h = rms_norm(x, pre_ffn_g[l])
        if l % 2 == 0:
            i = l // 2
            y = swiglu(h, ffn_w1[i], ffn_w3[i], ffn_w2[i])
        else:
            i = l // 2
            y = moe_swiglu(h, router_w[i], router_b[i], moe_w1[i], moe_w3[i], moe_w2[i])
        x = x + rms_norm(y, post_ffn_g[l])
    return x


_drawn_inputs = setup_inputs


def setup_inputs(seed=0):
    import zlib

    import numpy as np

    out = dict(_drawn_inputs(seed))
    spreads = {}
    factors = {}
    for name, (base, spread) in spreads.items():
        noise = np.random.default_rng([zlib.crc32(name.encode()), seed]).standard_normal(out[name].shape)
        drawn = base * np.exp(spread * noise) if base else spread * noise
        out[name] = __import__('jax').numpy.asarray(drawn.astype(out[name].dtype))
    for name, factor in factors.items():
        out[name] = (out[name] * factor).astype(out[name].dtype)
    return out
```

```python
from contextlib import ExitStack

import numpy as np

import concourse.bass as bass
from concourse import mybir

P = 128
D = 1024
SEQ = 256
NT = SEQ // P
KD = D // P
DEPTH = 2
FW = 512
NG = 4
D_IN = 3 * FW + 2 * D
FF = 2816
NE = 8
FE = 3584
RMS_EPS = 1e-6
LN_EPS = 1e-5

CW = 512
UNIT = 2048
RAW = 6
SPLIT = 3
GW = 256
GD = FF // GW
GE = FE // GW
MIX_UNITS = 2 * (D_IN // CW) + 2 + 2 + 4
DENSE_UNITS = 3 * GD
EXPERT_UNITS = 3 * GE
MIX_AT = (0, MIX_UNITS + DENSE_UNITS)
DENSE_AT = MIX_UNITS
MOE_AT = 2 * MIX_UNITS + DENSE_UNITS
ROUND_UNITS = NE * EXPERT_UNITS
assert EXPERT_UNITS % RAW == 0 and RAW % SPLIT == 0 and ROUND_UNITS % RAW == 0

F32 = mybir.dt.float32
F32R = mybir.dt.float32r
I32 = mybir.dt.int32
ALU = mybir.AluOpType
ACT = mybir.ActivationFunctionType
AX = mybir.AxisListType.X

C_SEQ = 0
C_CH = C_SEQ + NT * 2 * SEQ
C_ID = C_CH + 2 * P
C_IOTA = C_ID + P
C_TRI = C_IOTA + P
C_ONES = C_TRI + P
C_LOWER = C_ONES + P
C_ALL = C_LOWER + NE * NE


def build(nc, x, units_a, units_b, consts, gains, ln_gb, w_spatial, b_spatial, router_w, router_b, out):
    with ExitStack() as ctx:
        def sb(name, shape, dt):
            return ctx.enter_context(nc.sbuf_tensor(name, shape, dt))

        def sem(name):
            return ctx.enter_context(nc.semaphore(name))

        raw = sb("raw", [P, RAW, UNIT], F32)
        w_hi = sb("w_hi", [P, SPLIT, UNIT], F32R)
        w_lo = sb("w_lo", [P, SPLIT, UNIT], F32R)
        x_res = sb("x_res", [P, NT, D], F32)
        xn = sb("xn", [P, NT, D], F32)
        hT_hi = sb("hT_hi", [P, KD, SEQ], F32R)
        hT_lo = sb("hT_lo", [P, KD, SEQ], F32R)
        tok_hi = sb("tok_hi", [P, NT * D], F32R)
        tok_lo = sb("tok_lo", [P, NT * D], F32R)
        gT_hi = sb("gT_hi", [P, 2, 2, SEQ], F32R)
        gT_lo = sb("gT_lo", [P, 2, 2, SEQ], F32R)
        gates = sb("gates", [P, 2, NT, D], F32)
        zbuf = sb("zbuf", [P, 3, NT, FW], F32)
        gain_pre = sb("gain_pre", [P, D], F32)
        gain_post = sb("gain_post", [P, D], F32)
        cst = sb("cst", [P, C_ALL], F32)
        ident_r = sb("ident_r", [P, P], F32R)
        wsT = sb("wsT", [P, NG, P], F32)
        junk = sb("junk", [P, CW], F32)
        ws = sb("ws", [P, NG, P], F32)
        bs = sb("bs", [P, DEPTH, NG], F32)
        rw = sb("rw", [P, KD, NE], F32)
        rw_hi = sb("rw_hi", [P, KD, NE], F32R)
        rw_lo = sb("rw_lo", [P, KD, NE], F32R)
        rb = sb("rb", [P, NE], F32)
        S = sb("S", [P, NT, P], F32R)
        ST = sb("ST", [P, SEQ], F32R)
        sq = sb("sq", [P, 4], F32)
        st = sb("st", [P, 8, NT], F32)
        bnst = sb("bnst", [P, NT, 6], F32)
        bnag = sb("bnag", [P, NT, 2], F32)
        lg = sb("lg", [P, NT, NE], F32)
        cmp_a = sb("cmp_a", [P, NE, NE], F32)
        cmp_b = sb("cmp_b", [P, NE, NE], F32)
        rank = sb("rank", [P, NT, NE], F32)
        mask = sb("mask", [P, NT, NE], F32)
        gate = sb("gate", [P, NT, NE], F32)
        pos = sb("pos", [P, NT, NE + 1], F32)
        pos2 = sb("pos2", [P, NT, NE + 1], F32)
        rt = sb("rt", [P, 8, NT], F32)
        again = sb("again", [P, 1], I32)

        za, u_act, v_act = zbuf[:, 0], zbuf[:, 1], zbuf[:, 2]
        seqU = xn[:, :, :].rearrange("p t d -> p (t d)").rearrange("p (g n) -> p g n", g=NG)
        faT_hi = tok_hi[:, 0:D].rearrange("p (g s) -> p g s", g=NG)
        faT_lo = tok_lo[:, 0:D].rearrange("p (g s) -> p g s", g=NG)
        sgT_hi = tok_hi[:, D:2 * D].rearrange("p (g s) -> p g s", g=NG)
        sgT_lo = tok_lo[:, D:2 * D].rearrange("p (g s) -> p g s", g=NG)
        silu = zbuf[:, 0].rearrange("p t n -> p (t n)").rearrange("p (b t n) -> p b t n", b=2, t=NT)
        hid = zbuf[:, 1].rearrange("p t n -> p (t n)").rearrange("p (b t n) -> p b t n", b=2, t=NT)
        acc = gates[:, 0]
        ident = cst[:, C_ID:C_ID + P]
        iota = cst[:, C_IOTA:C_IOTA + P]
        xg_hi = tok_hi[:, :].rearrange("p (t d) -> p t d", t=NT)
        xg_lo = tok_lo[:, :].rearrange("p (t d) -> p t d", t=NT)
        yh = hT_hi[:, :, P:2 * P]
        yl = hT_lo[:, :, P:2 * P]

        bank = [ctx.enter_context(nc.psum_tensor(f"bank{i}", [P, CW], F32)) for i in range(8)]

        x_loaded = sem("x_loaded")
        cst_loaded = sem("cst_loaded")
        small_loaded = sem("small_loaded")
        pre_loaded = sem("pre_loaded")
        post_loaded = sem("post_loaded")
        ws_loaded = sem("ws_loaded")
        unit_landed = [sem(f"unit_landed{i}") for i in range(RAW)]
        hi_ready = sem("hi_ready")
        lo_ready = sem("lo_ready")
        unit_used = sem("unit_used")
        sq_done = sem("sq_done")
        x_ready = sem("x_ready")
        xn_ready = sem("xn_ready")
        hT_ps = sem("hT_ps")
        hT_hi_ok = sem("hT_hi_ok")
        hT_lo_ok = sem("hT_lo_ok")
        z_out = sem("z_out")
        wsT_ps = sem("wsT_ps")
        wsT_ok = sem("wsT_ok")
        fa_ps = sem("fa_ps")
        fa_out = sem("fa_out")
        fb_ps = sem("fb_ps")
        fb_hi = sem("fb_hi")
        fb_lo = sem("fb_lo")
        ln_ok = sem("ln_ok")
        sp_ps = sem("sp_ps")
        sg_ok = sem("sg_ok")
        sgT_ps = sem("sgT_ps")
        sgT_h = sem("sgT_h")
        sgT_l = sem("sgT_l")
        gated = sem("gated")
        merged = sem("merged")
        silu_ok = sem("silu_ok")
        hid_ok = sem("hid_ok")
        gT_ps = sem("gT_ps")
        gT_h = sem("gT_h")
        gT_l = sem("gT_l")
        rw_h = sem("rw_h")
        rw_l = sem("rw_l")
        id_ok = sem("id_ok")
        logit_ps = sem("logit_ps")
        shifted = sem("shifted")
        exp_ok = sem("exp_ok")
        mask_ok = sem("mask_ok")
        count_ps = sem("count_ps")
        xg_h = sem("xg_h")
        xg_l = sem("xg_l")
        route_ok = sem("route_ok")
        S_ok = sem("S_ok")
        pick_ps = sem("pick_ps")
        pick_h = sem("pick_h")
        pick_l = sem("pick_l")
        ST_ps = sem("ST_ps")
        ST_ok = sem("ST_ok")
        y_h = sem("y_h")
        y_l = sem("y_l")
        back_ps = sem("back_ps")
        acc_ok = sem("acc_ok")
        dve_step = sem("dve_step")
        summed = sem("summed")
        stored = sem("stored")

        block = ctx.enter_context(nc.Block())

        def over_groups(eng, groups, peel, step):
            for g in range(peel):
                step(g, g, 0)
            with eng.Fori(0, (groups - peel) // 2) as i:
                for j in range(2):
                    step(i * 2 + (peel + j), peel + j, i)

        def step_unit(g, like):
            return g * 3 - 2 if like >= 2 else g * 2

        @block.sync
        def _(sp):
            for t in range(NT):
                sp.dma_start(x_res[:, t, :], x[t * P:(t + 1) * P, :]).then_inc(x_loaded, 16)

            def load(u, slot, source):
                sp.dma_start(raw[:, slot, :], source).then_inc(unit_landed[slot], 16)

            for u in range(RAW):
                load(u, u, units_a[u])
            for first, count, source in ((RAW, MOE_AT - RAW, units_a[RAW:MOE_AT]), (MOE_AT, ROUND_UNITS, units_b)):
                turns = count // RAW
                with sp.Fori(0, turns) as i:
                    for s in range(RAW):
                        sp.wait_ge(lo_ready, i * RAW + (first + s - RAW + 1))
                        load(None, (first + s) % RAW, source[i * RAW + s])
                for s in range(turns * RAW, count):
                    sp.wait_ge(lo_ready, first + s - RAW + 1)
                    load(None, (first + s) % RAW, source[s])
            sp.wait_ge(route_ok, 1)
            more = sp.value_load(again[0:1, 0:1], min_val=0, max_val=1)
            with sp.If(more > 0):
                first = MOE_AT + ROUND_UNITS
                with sp.Fori(0, ROUND_UNITS // RAW) as i:
                    for s in range(RAW):
                        sp.wait_ge(lo_ready, i * RAW + (first + s - RAW + 1))
                        load(None, (first + s) % RAW, units_b[i * RAW + s])
            for t in range(NT):
                sp.wait_ge(x_ready, 4 * 3 + 2 * (t + 1))
                sp.dma_start(out[t * P:(t + 1) * P, :], x_res[:, t, :]).then_inc(stored, 16)
            sp.wait_ge(stored, 16 * NT)

        @block.gpsimd
        def _(pool):
            pool.dma_start(gain_pre[:, :], gains[0:1, :].partition_broadcast(P)).then_inc(pre_loaded, 16)
            pool.dma_start(cst[:, :], consts).then_inc(cst_loaded, 16)
            pool.dma_start(ws[:, :, :], w_spatial[0]).then_inc(ws_loaded, 16)
            pool.dma_start(gain_post[:, :], gains[1:2, :].partition_broadcast(P)).then_inc(post_loaded, 16)
            pool.dma_start(bs[:, :, :], b_spatial).then_inc(small_loaded, 16)
            pool.dma_start(rw[:, :, :], router_w).then_inc(small_loaded, 16)
            pool.dma_start(rb[:, :], router_b.partition_broadcast(P)).then_inc(small_loaded, 16)
            pool.wait_ge(xn_ready, NT)
            pool.dma_start(gain_pre[:, :], ln_gb[0:1, :].partition_broadcast(P)).then_inc(pre_loaded, 16)
            pool.wait_ge(wsT_ps, 1)
            pool.dma_start(ws[:, :, :], w_spatial[1]).then_inc(ws_loaded, 16)
            for l in range(DEPTH):
                pool.wait_ge(ln_ok, NT * (l + 1))
                pool.dma_start(gain_pre[:, :], gains[4 * l + 2:4 * l + 3, :].partition_broadcast(P))\
                    .then_inc(pre_loaded, 16)
                pool.wait_ge(x_ready, 4 * (2 * l + 1))
                pool.dma_start(gain_post[:, :], gains[4 * l + 3:4 * l + 4, :].partition_broadcast(P))\
                    .then_inc(post_loaded, 16)
                if l == 0:
                    pool.wait_ge(xn_ready, 2 * NT)
                    pool.dma_start(gain_pre[:, :], gains[4:5, :].partition_broadcast(P)).then_inc(pre_loaded, 16)
                    pool.wait_ge(x_ready, 8)
                    pool.dma_start(gain_post[:, :], gains[5:6, :].partition_broadcast(P)).then_inc(post_loaded, 16)
                    pool.wait_ge(xn_ready, 3 * NT)
                    pool.dma_start(gain_pre[:, :], ln_gb[1:2, :].partition_broadcast(P)).then_inc(pre_loaded, 16)

        @block.scalar
        def _(act):
            def hi(u, like=None, turns=0):
                like = u if like is None else like
                act.wait_ge(unit_landed[like % RAW], turns * 16 + 16 * (like // RAW + 1))
                if not isinstance(u, int) or u >= SPLIT:
                    act.wait_ge(unit_used, u - SPLIT + 1)
                nc.scalar.activation(w_hi[:, like % SPLIT, :], raw[:, like % RAW, :], ACT.Copy).then_inc(hi_ready, 1)

            def squares(source, n):
                for q in range(4):
                    if n or q:
                        act.wait_ge(sq_done, 4 * n + q)
                    nc.scalar.activation(junk[:, :], source(q), ACT.Square, accum_out=sq[:, q:q + 1])\
                        .then_inc(sq_done, 1)

            def evict_hT(n):
                for b in range(4):
                    act.wait_ge(hT_ps, 4 * n + b + 1)
                    nc.scalar.activation(hT_hi[:, 2 * b:2 * b + 2, :], bank[b][:, :], ACT.Copy).then_inc(hT_hi_ok, 1)

            def quarter(q):
                return x_res[:, q // 2, (q % 2) * CW:(q % 2 + 1) * CW]

            def pre_norm(n, m, ahead=None):
                if n:
                    act.wait_ge(x_ready, 2 * n)
                else:
                    act.wait_ge(x_loaded, 16 * NT)
                squares(quarter, n)
                if ahead is not None:
                    hi(ahead)
                evict_hT(m)

            def post_norm(n, source=None):
                if n == 7:
                    act.wait_ge(summed, 1)
                else:
                    act.wait_ge(unit_used, (MIX_UNITS, MIX_UNITS + DENSE_UNITS, MOE_AT)[n // 2])
                squares(source or (lambda q: bank[4 + q][:, :]), n)

            def mixer(l):
                at = MIX_AT[l]
                pre_norm(4 * l, 3 * l, at + 2)
                for c in range(7):
                    hi(at + 2 * c + 3)
                    act.wait_ge(unit_used, at + 2 * c + 2)
                    for t in range(NT):
                        src = bank[2 * (c % 2) + t][:, :]
                        if c == 0:
                            dst, fn = za[:, t, :], ACT.Copy
                        elif c == 1:
                            dst, fn = v_act[:, t, :], ACT.Gelu
                        elif c == 2:
                            dst, fn = u_act[:, t, :], ACT.Gelu
                        else:
                            h = (c - 3) % 2
                            dst, fn = gates[:, (c - 3) // 2, t, h * CW:(h + 1) * CW], ACT.Sigmoid
                        nc.scalar.activation(dst, src, fn).then_inc(z_out, 1)
                    hi(at + 2 * c + 4)
                    if c == 4:
                        for b in range(2):
                            act.wait_ge(fb_ps, 2 * l + b + 1)
                            nc.scalar.activation(faT_hi[:, 2 * b:2 * b + 2, :], bank[6 + b][:, :], ACT.Copy)\
                                .then_inc(fb_hi, 1)
                    if c == 6:
                        for b in range(2):
                            act.wait_ge(sgT_ps, 2 * l + b + 1)
                            nc.scalar.activation(sgT_hi[:, 2 * b:2 * b + 2, :], bank[6 + b][:, :], ACT.Copy)\
                                .then_inc(sgT_h, 1)
                for u in range(at + 17, at + 21):
                    hi(u)
                evict_hT(3 * l + 1)
                for u in range(at + 21, at + 24):
                    hi(u)
                post_norm(4 * l + 1)

            def swiglu(u0, like0, turns0, q0, groups, peel, nt):
                def step(g, like, turns):
                    s, sl = step_unit(g, like), step_unit(like, like)
                    par = like % 2
                    if like or nt == 1:
                        hi(u0 + (s + 2), like0 + sl + 2, turns0 + turns)
                    if like >= 1:
                        act.wait_ge(gT_ps, q0 + g)
                        nc.scalar.activation(gT_hi[:, 1 - par, :, 0:nt * P],
                                             bank[2 + 1 - par][:, 0:2 * nt * P].rearrange("p (f s) -> p f s", f=2),
                                             ACT.Copy).then_inc(gT_h, 1)
                    hi(u0 + (s + 3), like0 + sl + 3, turns0 + turns)
                    act.wait_ge(unit_used, u0 + (s + 2))
                    for t in range(nt):
                        src = bank[t if nt == NT else par][:, 0:GW]
                        nc.scalar.activation(silu[:, par, t, :], src, ACT.Silu).then_inc(silu_ok, NT // nt)
                    if like >= 2:
                        hi(u0 + (s + 4), like0 + sl + 4, turns0 + turns)

                over_groups(act, groups, peel, step)
                par = (groups - 1) % 2
                act.wait_ge(gT_ps, q0 + groups)
                nc.scalar.activation(gT_hi[:, par, :, 0:nt * P],
                                     bank[2 + par][:, 0:2 * nt * P].rearrange("p (f s) -> p f s", f=2),
                                     ACT.Copy).then_inc(gT_h, 1)

            def evict_pick(m):
                act.wait_ge(pick_ps, m + 1)
                for b in range(2):
                    nc.scalar.activation(hT_hi[:, 4 * b:4 * b + 4, 0:P],
                                         bank[6 + b][:, :].rearrange("p (k s) -> p k s", k=4),
                                         ACT.Copy).then_inc(pick_h, 1)

            def expert(r, e, last):
                n = e + NE * r
                act.wait_ge(ST_ps, n + 1)
                nc.scalar.activation(ST[:, :], bank[6][:, 0:SEQ], ACT.Copy).then_inc(ST_ok, 1)
                u0 = n * EXPERT_UNITS + MOE_AT
                swiglu(u0, MOE_AT, n * (EXPERT_UNITS // RAW), n * GE + GD, GE, 4, 1)
                if not last:
                    for i in range(SPLIT - 1):
                        hi(u0 + (EXPERT_UNITS + i), MOE_AT + EXPERT_UNITS + i, n * (EXPERT_UNITS // RAW))
                evict_pick(e + (r * (NE + 1) + 1))
                act.wait_ge(unit_used, u0 + EXPERT_UNITS)
                for h in range(2):
                    nc.scalar.activation(yh[:, 4 * h:4 * h + 4, :],
                                         bank[4 + h][:, :].rearrange("p (k s) -> p k s", k=4),
                                         ACT.Copy).then_inc(y_h, 1)

            def moe_round(r):
                evict_pick(r * (NE + 1))
                with act.Fori(0, NE - 1) as e:
                    expert(r, e, False)
                expert(r, NE - 1, True)

            for u in range(SPLIT - 1):
                hi(u)
            mixer(0)
            pre_norm(2, 2, DENSE_AT + 2)
            swiglu(DENSE_AT, DENSE_AT, 0, 0, GD, 3, NT)
            hi(MIX_AT[1])
            hi(MIX_AT[1] + 1)
            post_norm(3)
            mixer(1)
            pre_norm(6, 5)
            act.wait_ge(cst_loaded, 16)
            nc.scalar.activation(ident_r[:, :], ident, ACT.Copy).then_inc(id_ok, 1)
            act.wait_ge(small_loaded, 48)
            nc.scalar.activation(rw_hi[:, :, :], rw[:, :, :], ACT.Copy).then_inc(rw_h, 1)
            act.wait_ge(xn_ready, 4 * NT)
            for t in range(NT):
                nc.scalar.activation(xg_hi[:, t, :], xn[:, t, :], ACT.Copy).then_inc(xg_h, 1)
            act.wait_ge(shifted, 1)
            nc.scalar.activation(gate[:, :, :], lg[:, :, :], ACT.Exp).then_inc(exp_ok, 1)
            act.wait_ge(route_ok, 1)
            more = act.value_load(again[0:1, 0:1], min_val=0, max_val=1)
            moe_round(0)
            with act.If(more > 0):
                for u in range(SPLIT - 1):
                    hi(MOE_AT + ROUND_UNITS + u)
                moe_round(1)
            post_norm(7, lambda q: acc[:, q // 2, (q % 2) * CW:(q % 2 + 1) * CW])

        @block.vector
        def _(dve):
            own = [0]

            def link(instruction):
                own[0] += 1
                instruction.then_inc(dve_step, 1)
                dve.wait_ge(dve_step, own[0])

            def lo(u, like=None):
                like = u if like is None else like
                dve.wait_ge(hi_ready, u + 1)
                nc.vector.tensor_tensor(w_lo[:, like % SPLIT, :], raw[:, like % RAW, :],
                                        w_hi[:, like % SPLIT, :].bitcast(F32), ALU.subtract).then_inc(lo_ready, 1)

            def rsqrt(dst, v, tmp, half):
                link(nc.vector.tensor_scalar(half, v, -0.5, None, ALU.mult))
                link(nc.vector.tensor_scalar(tmp.bitcast(I32), v.bitcast(I32), 1, None, ALU.logical_shift_right))
                link(nc.vector.tensor_scalar(dst.bitcast(I32), tmp.bitcast(I32), -1.0, float(0x5F3759DF),
                                             ALU.mult, ALU.add))
                for _ in range(4):
                    link(nc.vector.tensor_tensor(tmp, dst, dst, ALU.mult))
                    link(nc.vector.tensor_tensor(tmp, tmp, half, ALU.mult))
                    link(nc.vector.scalar_tensor_tensor(dst, tmp, 1.5, dst, ALU.add, ALU.mult))

            def rms(n):
                dve.wait_ge(sq_done, 4 * (n + 1))
                pairs = sq[:, :].rearrange("p (t h) -> p t h", t=NT)
                link(nc.vector.tensor_tensor(st[:, 0, :], pairs[:, :, 0], pairs[:, :, 1], ALU.add))
                link(nc.vector.tensor_scalar(st[:, 1, :], st[:, 0, :], 1.0 / D, RMS_EPS, ALU.mult, ALU.add))
                rsqrt(st[:, 2, :], st[:, 1, :], st[:, 3, :], st[:, 0, :])

            def evict_hT(n):
                for b in range(4):
                    dve.wait_ge(hT_hi_ok, 4 * n + b + 1)
                    nc.vector.tensor_tensor(hT_lo[:, 2 * b:2 * b + 2, :],
                                            bank[b][:, :].rearrange("p (k s) -> p k s", k=2),
                                            hT_hi[:, 2 * b:2 * b + 2, :].bitcast(F32), ALU.subtract)\
                        .then_inc(hT_lo_ok, 1)

            def pre_norm(n, m, load, ahead=None):
                rms(n)
                dve.wait_ge(pre_loaded, 16 * load)
                for t in range(NT):
                    nc.vector.scalar_tensor_tensor(xn[:, t, :], x_res[:, t, :], st[:, 2, t:t + 1], gain_pre[:, :],
                                                   ALU.mult, ALU.mult).then_inc(xn_ready, 1)
                if ahead is not None:
                    lo(ahead)
                evict_hT(m)

            def post_norm(n, source=None):
                rms(n)
                dve.wait_ge(post_loaded, 16 * ((n + 1) // 2))
                for t in range(NT):
                    for h in range(2):
                        cols = slice(h * CW, (h + 1) * CW)
                        src = source(t, h) if source else bank[4 + 2 * t + h][:, :]
                        ins = nc.vector.scalar_tensor_tensor(xn[:, t, cols], src, st[:, 2, t:t + 1],
                                                             gain_post[:, cols], ALU.mult, ALU.mult)
                        link(ins)
                        nc.vector.tensor_tensor(x_res[:, t, cols], x_res[:, t, cols], xn[:, t, cols], ALU.add)\
                            .then_inc(x_ready, 1)

            def mixer(l):
                at = MIX_AT[l]
                dve.wait_ge(wsT_ps, l + 1)
                nc.vector.tensor_copy(wsT[:, :, :], bank[7][:, :].rearrange("p (g q) -> p g q", g=NG))\
                    .then_inc(wsT_ok, 1)
                pre_norm(4 * l, 3 * l, 3 * l + 1, at + 2)
                for c in range(7):
                    if c == 3:
                        for g in range(NG):
                            dve.wait_ge(fa_ps, NG * l + g + 1)
                            nc.vector.tensor_copy(seqU[:, g, :], bank[4 + g % 2][:, :]).then_inc(fa_out, 1)
                    lo(at + 2 * c + 3)
                    if c == 2:
                        dve.wait_ge(z_out, 14 * l + 4)
                        for t in range(NT):
                            link(nc.vector.bn_stats(bnst[:, t, :], v_act[:, t, :]))
                            link(nc.vector.bn_aggr(bnag[:, t, :], bnst[:, t, :]))
                        link(nc.vector.tensor_scalar(st[:, 4, :], bnag[:, :, 1], LN_EPS, None, ALU.add))
                        rsqrt(st[:, 5, :], st[:, 4, :], st[:, 6, :], st[:, 7, :])
                        dve.wait_ge(pre_loaded, 16 * (3 * l + 2))
                        for t in range(NT):
                            link(nc.vector.tensor_scalar(v_act[:, t, :], v_act[:, t, :], bnag[:, t, 0:1],
                                                         st[:, 5, t:t + 1], ALU.subtract, ALU.mult))
                            link(nc.vector.tensor_tensor(v_act[:, t, :], v_act[:, t, :], gain_pre[:, 0:FW], ALU.mult))
                            nc.vector.tensor_tensor(v_act[:, t, :], v_act[:, t, :], gain_pre[:, FW:2 * FW], ALU.add)\
                                .then_inc(ln_ok, 1)
                    if c == 5:
                        for b in range(2):
                            dve.wait_ge(fb_hi, 2 * l + b + 1)
                            nc.vector.tensor_tensor(faT_lo[:, 2 * b:2 * b + 2, :],
                                                    bank[6 + b][:, :].rearrange("p (k s) -> p k s", k=2),
                                                    faT_hi[:, 2 * b:2 * b + 2, :].bitcast(F32), ALU.subtract)\
                                .then_inc(fb_lo, 1)
                    if c == 6:
                        dve.wait_ge(z_out, 14 * l + 6)
                        dve.wait_ge(small_loaded, 48)
                        for t in range(NT):
                            dve.wait_ge(sp_ps, NT * l + t + 1)
                            for g in range(NG):
                                cols = slice(g * P, (g + 1) * P)
                                nc.vector.scalar_tensor_tensor(u_act[:, t, cols], bank[4 + t][:, cols],
                                                               bs[:, l, g:g + 1], u_act[:, t, cols],
                                                               ALU.add, ALU.mult).then_inc(sg_ok, 1)
                    lo(at + 2 * c + 4)
                for b in range(2):
                    dve.wait_ge(sgT_h, 2 * l + b + 1)
                    nc.vector.tensor_tensor(sgT_lo[:, 2 * b:2 * b + 2, :],
                                            bank[6 + b][:, :].rearrange("p (k s) -> p k s", k=2),
                                            sgT_hi[:, 2 * b:2 * b + 2, :].bitcast(F32), ALU.subtract)\
                        .then_inc(sgT_l, 1)
                lo(at + 17)
                for b in range(2):
                    for h in range(2):
                        cols = slice(h * CW, (h + 1) * CW)
                        dve.wait_ge(z_out, 14 * (l + 1))
                        dve.wait_ge(unit_used, at + 14 + 2 * b + h + 1)
                        for t in range(NT):
                            nc.vector.tensor_tensor(gates[:, b, t, cols], gates[:, b, t, cols],
                                                    bank[4 * b + 2 * t + h][:, :], ALU.mult).then_inc(gated, 1)
                            if b:
                                dve.wait_ge(gated, 8 * l + 4 + 2 * h + t + 1)
                                nc.vector.tensor_tensor(gates[:, 0, t, cols], gates[:, 0, t, cols],
                                                        gates[:, 1, t, cols], ALU.add).then_inc(merged, 1)
                        if not b or not h:
                            lo(at + 18 + 2 * b + h)
                evict_hT(3 * l + 1)
                for u in range(at + 21, at + 24):
                    lo(u)
                post_norm(4 * l + 1)

            def rest(par, nt):
                nc.vector.tensor_tensor(gT_lo[:, par, :, 0:nt * P],
                                        bank[2 + par][:, 0:2 * nt * P].rearrange("p (f s) -> p f s", f=2),
                                        gT_hi[:, par, :, 0:nt * P].bitcast(F32), ALU.subtract).then_inc(gT_l, 1)

            def swiglu(u0, like0, q0, groups, peel, nt):
                def step(g, like, turns):
                    s, sl = step_unit(g, like), step_unit(like, like)
                    par = like % 2
                    if like or nt == 1:
                        lo(u0 + (s + 2), like0 + sl + 2)
                    if like >= 1:
                        dve.wait_ge(gT_h, q0 + g)
                        rest(1 - par, nt)
                    lo(u0 + (s + 3), like0 + sl + 3)
                    dve.wait_ge(silu_ok, (q0 + (g + 1)) * NT)
                    for t in range(nt):
                        src = bank[t if nt == NT else par][:, GW:2 * GW]
                        nc.vector.tensor_tensor(hid[:, par, t, :], src, silu[:, par, t, :], ALU.mult)\
                            .then_inc(hid_ok, NT // nt)
                    if like >= 2:
                        lo(u0 + (s + 4), like0 + sl + 4)

                over_groups(dve, groups, peel, step)

            def last_rest(q, par, nt):
                dve.wait_ge(gT_h, q)
                rest(par, nt)

            def one_hot(r, e):
                table = (pos, pos2)[r]
                for t in range(NT):
                    nc.vector.tensor_scalar(S[:, t, :], iota, table[:, t, bass.ds(e, 1)], None, ALU.is_equal)\
                        .then_inc(S_ok, 1)

            def evict_pick(m):
                for b in range(2):
                    dve.wait_ge(pick_h, (m * 2) + (b + 1))
                    nc.vector.tensor_tensor(hT_lo[:, 4 * b:4 * b + 4, 0:P],
                                            bank[6 + b][:, :].rearrange("p (k s) -> p k s", k=4),
                                            hT_hi[:, 4 * b:4 * b + 4, 0:P].bitcast(F32), ALU.subtract)\
                        .then_inc(pick_l, 1)

            def expert(r, e, last):
                n = e + NE * r
                u0 = n * EXPERT_UNITS + MOE_AT
                swiglu(u0, MOE_AT, n * GE + GD, GE, 4, 1)
                one_hot(r, e + 1)
                last_rest(n * GE + (GD + GE), (GE - 1) % 2, 1)
                if not last:
                    for i in range(SPLIT - 1):
                        lo(u0 + (EXPERT_UNITS + i), MOE_AT + EXPERT_UNITS + i)
                evict_pick(e + (r * (NE + 1) + 1))
                for h in range(2):
                    dve.wait_ge(y_h, (n * 2) + (h + 1))
                    nc.vector.tensor_tensor(yl[:, 4 * h:4 * h + 4, :],
                                            bank[4 + h][:, :].rearrange("p (k s) -> p k s", k=4),
                                            yh[:, 4 * h:4 * h + 4, :].bitcast(F32), ALU.subtract).then_inc(y_l, 1)
                dve.wait_ge(acc_ok, n * 4 + 1)
                for t in range(NT):
                    dve.wait_ge(back_ps, n * NT + (t + 1))
                    for h in range(2):
                        cols = slice(h * CW, (h + 1) * CW)
                        nc.vector.scalar_tensor_tensor(acc[:, t, cols], bank[2 * t + h][:, :],
                                                       gate[:, t, bass.ds(e, 1)], acc[:, t, cols],
                                                       ALU.mult, ALU.add).then_inc(acc_ok, 1)

            def moe_round(r):
                one_hot(r, 0)
                evict_pick(r * (NE + 1))
                with dve.Fori(0, NE - 1) as e:
                    expert(r, e, False)
                expert(r, NE - 1, True)
                dve.wait_ge(acc_ok, 4 * NE * (r + 1) + 1)

            def route():
                dve.wait_ge(rw_h, 1)
                nc.vector.tensor_tensor(rw_lo[:, :, :], rw[:, :, :], rw_hi[:, :, :].bitcast(F32), ALU.subtract)\
                    .then_inc(rw_l, 1)
                for t in range(NT):
                    dve.wait_ge(xg_h, t + 1)
                    nc.vector.tensor_tensor(xg_lo[:, t, :], xn[:, t, :], xg_hi[:, t, :].bitcast(F32), ALU.subtract)\
                        .then_inc(xg_l, 1)
                nc.vector.memset(acc, 0.0).then_inc(acc_ok, 1)
                dve.wait_ge(logit_ps, 1)
                for t in range(NT):
                    link(nc.vector.tensor_tensor(lg[:, t, :], bank[4][:, t * NE:(t + 1) * NE], rb[:, :], ALU.add))
                for t in range(NT):
                    over_e = lg[:, t, :].unsqueeze(1).broadcast_to([P, NE, NE])
                    by_e = lg[:, t, :].unsqueeze(2).broadcast_to([P, NE, NE])
                    link(nc.vector.tensor_tensor(cmp_a[:, :, :], over_e, by_e, ALU.is_gt))
                    link(nc.vector.tensor_tensor(cmp_b[:, :, :], over_e, by_e, ALU.is_equal))
                    link(nc.vector.tensor_tensor(cmp_b[:, :, :], cmp_b[:, :, :],
                                                 cst[:, C_LOWER:C_ALL].rearrange("p (e f) -> p e f", e=NE), ALU.mult))
                    link(nc.vector.tensor_tensor(cmp_a[:, :, :], cmp_a[:, :, :], cmp_b[:, :, :], ALU.add))
                    link(nc.vector.tensor_reduce(rank[:, t, :], cmp_a[:, :, :], AX, ALU.add))
                nc.vector.tensor_scalar(mask[:, :, :], rank[:, :, :], 1.5, None, ALU.is_lt).then_inc(mask_ok, 1)
                link(nc.vector.tensor_reduce(rt[:, 0, :], lg[:, :, :], AX, ALU.max))
                for t in range(NT):
                    link(nc.vector.tensor_scalar(lg[:, t, :], lg[:, t, :], rt[:, 0, t:t + 1], None, ALU.subtract))
                nc.vector.tensor_copy(rt[:, 1, :], rt[:, 0, :]).then_inc(shifted, 1)
                dve.wait_ge(exp_ok, 1)
                dve.wait_ge(mask_ok, 1)
                link(nc.vector.tensor_tensor(gate[:, :, :], gate[:, :, :], mask[:, :, :], ALU.mult))
                link(nc.vector.tensor_reduce(rt[:, 2, :], gate[:, :, :], AX, ALU.add))
                link(nc.vector.reciprocal(rt[:, 3, :], rt[:, 2, :]))
                for t in range(NT):
                    link(nc.vector.tensor_scalar(gate[:, t, :], gate[:, t, :], rt[:, 3, t:t + 1], None, ALU.mult))
                dve.wait_ge(count_ps, 1)
                link(nc.vector.memset(pos[:, :, :], -1.0))
                link(nc.vector.tensor_tensor(pos[:, :, 0:NE],
                                             bank[5][:, 0:NT * NE].rearrange("p (t e) -> p t e", t=NT),
                                             mask[:, :, :], ALU.mult))
                link(nc.vector.tensor_scalar(pos[:, :, 0:NE], pos[:, :, 0:NE], 1.0, None, ALU.subtract))
                link(nc.vector.tensor_scalar(pos2[:, :, :], pos[:, :, :], float(P), None, ALU.subtract))
                link(nc.vector.tensor_reduce(rt[:, 4, 0:1], bank[5][:, NT * NE:(NT + 1) * NE], AX, ALU.max))
                link(nc.vector.tensor_scalar(rt[:, 5, 0:1], rt[:, 4, 0:1], float(P), None, ALU.is_gt))
                nc.vector.tensor_copy(again[:, :], rt[:, 5, 0:1]).then_inc(route_ok, 1)

            for u in range(SPLIT - 1):
                lo(u)
            mixer(0)
            pre_norm(2, 2, 3, DENSE_AT + 2)
            swiglu(DENSE_AT, DENSE_AT, 0, GD, 3, NT)
            last_rest(GD, (GD - 1) % 2, NT)
            lo(MIX_AT[1])
            lo(MIX_AT[1] + 1)
            post_norm(3)
            mixer(1)
            pre_norm(6, 5, 6)
            route()
            dve.wait_ge(route_ok, 1)
            more = dve.value_load(again[0:1, 0:1], min_val=0, max_val=1)
            moe_round(0)
            with dve.If(more > 0):
                for u in range(SPLIT - 1):
                    lo(MOE_AT + ROUND_UNITS + u)
                moe_round(1)
            nc.vector.tensor_copy(rt[:, 6, :], rt[:, 3, :]).then_inc(summed, 1)
            post_norm(7, lambda t, h: acc[:, t, h * CW:(h + 1) * CW])

        @block.tensor
        def _(pe):
            def three(dst, xh, xl, wh, wl, start, stop):
                nc.tensor.matmul(dst, xh, wh, start=start, stop=False)
                nc.tensor.matmul(dst, xh, wl, start=False, stop=False)
                return nc.tensor.matmul(dst, xl, wh, start=False, stop=stop)

            def transpose_hT(m, source):
                for b in range(4):
                    for k in range(2):
                        for t in range(NT):
                            last = nc.tensor.transpose(bank[b][:, k * SEQ + t * P:k * SEQ + (t + 1) * P],
                                                       source(t, 2 * b + k), ident)
                    last.then_inc(hT_ps, 1)

            def pre_norm(n, m):
                if m == 0:
                    pe.wait_ge(cst_loaded, 16)
                pe.wait_ge(xn_ready, NT * (n + 1))
                transpose_hT(m, lambda t, k: xn[:, t, k * P:(k + 1) * P])

            def weights(slot, k):
                cols = slice(k * CW, (k + 1) * CW)
                return w_hi[:, slot % SPLIT, cols], w_lo[:, slot % SPLIT, cols]

            def mixer(l):
                at = MIX_AT[l]
                pe.wait_ge(ws_loaded, 16 * (l + 1))
                if l == 0:
                    pe.wait_ge(cst_loaded, 16)
                else:
                    pe.wait_ge(x_ready, 8)
                for g in range(NG):
                    last = nc.tensor.transpose(bank[7][:, g * P:(g + 1) * P], ws[:, g, :], ident)
                last.then_inc(wsT_ps, 1)
                pre_norm(2 * l, 3 * l)
                for c in range(7):
                    if c >= 2:
                        pe.wait_ge(z_out, 14 * l + 2 * (c - 1))
                    for h in range(2):
                        if c == 0:
                            pe.wait_ge(hT_lo_ok, 4 * (3 * l) + 4)
                        u = at + 2 * c + h
                        pe.wait_ge(lo_ready, u + 1)
                        for t in range(NT):
                            for i in range(4):
                                wh, wl = weights(u, i)
                                rows = slice(t * P, (t + 1) * P)
                                k = 4 * h + i
                                last = three(bank[2 * (c % 2) + t][:, :], hT_hi[:, k, rows], hT_lo[:, k, rows], wh, wl,
                                             k == 0, k == KD - 1)
                        last.then_inc(unit_used, 1)
                    if c == 2:
                        pe.wait_ge(z_out, 14 * l + 2)
                        for g in range(NG):
                            if g >= 2:
                                pe.wait_ge(fa_out, NG * l + g - 1)
                            for t in range(NT):
                                last = nc.tensor.matmul(bank[4 + g % 2][:, :], za[:, t, g * P:(g + 1) * P],
                                                        cst[:, C_SEQ + t * 2 * SEQ:C_SEQ + (t + 1) * 2 * SEQ],
                                                        start=t == 0, stop=t == NT - 1)
                            last.then_inc(fa_ps, 1)
                    if c == 3:
                        pe.wait_ge(fa_out, NG * (l + 1))
                        pe.wait_ge(wsT_ok, l + 1)
                        for g in range(NG):
                            dst = bank[6 + g // 2][:, (g % 2) * SEQ:(g % 2 + 1) * SEQ]
                            for i in range(2):
                                last = nc.tensor.matmul(dst, cst[:, C_CH + i * P:C_CH + (i + 1) * P],
                                                        seqU[:, g, i * SEQ:(i + 1) * SEQ], start=i == 0, stop=i == 1)
                            if g % 2:
                                last.then_inc(fb_ps, 1)
                    if c == 4:
                        for t in range(NT):
                            pe.wait_ge(ln_ok, NT * l + t + 1)
                            for g in range(NG):
                                last = nc.tensor.matmul(bank[4 + t][:, g * P:(g + 1) * P], wsT[:, g, :],
                                                        v_act[:, t, g * P:(g + 1) * P], start=True, stop=True)
                            last.then_inc(sp_ps, 1)
                pe.wait_ge(fb_lo, 2 * (l + 1))
                pe.wait_ge(sg_ok, NT * NG * (l + 1))
                for g in range(NG):
                    for t in range(NT):
                        last = nc.tensor.transpose(bank[6 + g // 2][:, (g % 2) * SEQ + t * P:(g % 2) * SEQ + (t + 1) * P],
                                                   u_act[:, t, g * P:(g + 1) * P], ident)
                    if g % 2:
                        last.then_inc(sgT_ps, 1)
                pe.wait_ge(z_out, 14 * (l + 1))
                for h in range(2):
                    u = at + 14 + h
                    pe.wait_ge(lo_ready, u + 1)
                    for t in range(NT):
                        for i in range(4):
                            wh, wl = weights(u, i)
                            rows = slice(t * P, (t + 1) * P)
                            last = three(bank[2 * t + h][:, :], faT_hi[:, i, rows], faT_lo[:, i, rows], wh, wl,
                                         i == 0, i == 3)
                    last.then_inc(unit_used, 1)
                pe.wait_ge(sgT_l, 2 * (l + 1))
                for h in range(2):
                    u = at + 16 + h
                    pe.wait_ge(lo_ready, u + 1)
                    for t in range(NT):
                        for i in range(4):
                            wh, wl = weights(u, i)
                            rows = slice(t * P, (t + 1) * P)
                            last = three(bank[4 + 2 * t + h][:, :], sgT_hi[:, i, rows], sgT_lo[:, i, rows], wh, wl,
                                         i == 0, i == 3)
                    last.then_inc(unit_used, 1)
                pe.wait_ge(gated, 8 * l + 4)
                for b in range(4):
                    if b % 2 == 0:
                        pe.wait_ge(merged, 4 * l + b + 2)
                    for k in range(2):
                        for t in range(NT):
                            c0 = (2 * b + k) * P
                            last = nc.tensor.transpose(bank[b][:, k * SEQ + t * P:k * SEQ + (t + 1) * P],
                                                       gates[:, 0, t, c0:c0 + P], ident)
                    last.then_inc(hT_ps, 1)
                pe.wait_ge(merged, 4 * (l + 1))
                for kh in range(2):
                    pe.wait_ge(hT_lo_ok, 4 * (3 * l + 1) + 2 * (kh + 1))
                    for h in range(2):
                        u = at + 18 + 2 * kh + h
                        pe.wait_ge(lo_ready, u + 1)
                        for t in range(NT):
                            for i in range(4):
                                wh, wl = weights(u, i)
                                rows = slice(t * P, (t + 1) * P)
                                k = 4 * kh + i
                                last = three(bank[4 + 2 * t + h][:, :], hT_hi[:, k, rows], hT_lo[:, k, rows], wh, wl,
                                             k == 0, k == KD - 1)
                        last.then_inc(unit_used, 1)

            def swiglu(u0, like0, q0, groups, peel, nt, between=None):
                def up(u, like, h, par):
                    pe.wait_ge(lo_ready, u + 1)
                    for t in range(nt):
                        dst = bank[t if nt == NT else par][:, :]
                        for i in range(4):
                            wh, wl = weights(like, i)
                            rows = slice(t * P, (t + 1) * P)
                            k = 4 * h + i
                            last = three(dst, hT_hi[:, k, rows], hT_lo[:, k, rows], wh, wl, k == 0, k == KD - 1)
                    last.then_inc(unit_used, 1)

                def turn(par):
                    for f in range(2):
                        for t in range(nt):
                            last = nc.tensor.transpose(bank[2 + par][:, (f * nt + t) * P:(f * nt + t + 1) * P],
                                                       hid[:, par, t, f * P:(f + 1) * P], ident)
                    last.then_inc(gT_ps, 1)

                def down(u, like, q, par, start, stop):
                    pe.wait_ge(gT_l, q + 1)
                    pe.wait_ge(lo_ready, u + 1)
                    for t in range(nt):
                        rows = slice(t * P, (t + 1) * P)
                        for f in range(2):
                            for h in range(2):
                                wh, wl = weights(like, 2 * f + h)
                                last = three(bank[4 + 2 * t + h][:, :], gT_hi[:, par, f, rows], gT_lo[:, par, f, rows],
                                             wh, wl, start and f == 0, stop and f == 1)
                    last.then_inc(unit_used, 1)

                def step(g, like, turns):
                    s, sl = step_unit(g, like), step_unit(like, like)
                    par = like % 2
                    back = 1 if nt == NT else 2
                    if like >= back:
                        pe.wait_ge(hid_ok, (q0 + (g + 1 - back)) * NT)
                    up(u0 + s, like0 + sl, 0, par)
                    if like >= 1:
                        pe.wait_ge(hid_ok, (q0 + g) * NT)
                        if like >= 3:
                            pe.wait_ge(gT_l, q0 + (g - 2))
                        turn(1 - par)
                    up(u0 + (s + 1), like0 + sl + 1, 1, par)
                    if like >= 2:
                        down(u0 + (s + 2), like0 + sl + 2, q0 + (g - 2), par, like == 2, False)

                over_groups(pe, groups, peel, step)
                par = (groups - 1) % 2
                down(u0 + (3 * groups - 2), like0 + 3 * groups - 2, q0 + (groups - 2), 1 - par, False, False)
                pe.wait_ge(hid_ok, (q0 + groups) * NT)
                turn(par)
                if between:
                    between()
                down(u0 + (3 * groups - 1), like0 + 3 * groups - 1, q0 + (groups - 1), par, False, True)

            def gather(m):
                pe.wait_ge(S_ok, (m + 1) * NT)
                for b in range(2):
                    for i in range(4):
                        k = 4 * b + i
                        cols = slice(k * P, (k + 1) * P)
                        dst = bank[6 + b][:, i * P:(i + 1) * P]
                        for t in range(NT):
                            nc.tensor.matmul(dst, xg_hi[:, t, cols], S[:, t, :], start=t == 0, stop=False)
                            last = nc.tensor.matmul(dst, xg_lo[:, t, cols], S[:, t, :], start=False, stop=t == NT - 1)
                last.then_inc(pick_ps, 1)

            def expert(r, e):
                n = e + NE * r
                m = e + r * (NE + 1)
                pe.wait_ge(pick_l, (m + 1) * 2)
                for t in range(NT):
                    last = nc.tensor.matmul(bank[6][:, t * P:(t + 1) * P], S[:, t, :], ident_r[:, :],
                                            start=True, stop=True)
                last.then_inc(ST_ps, 1)
                pe.wait_ge(acc_ok, n * 4 + 1)

                def gather_next():
                    pe.wait_ge(ST_ok, n + 1)
                    gather(m + 1)

                swiglu(n * EXPERT_UNITS + MOE_AT, MOE_AT, n * GE + GD, GE, 4, 1, gather_next)
                pe.wait_ge(y_l, (n + 1) * 2)
                for t in range(NT):
                    for h in range(2):
                        dst = bank[2 * t + h][:, :]
                        rows = slice(t * P, (t + 1) * P)
                        nc.tensor.matmul(dst, ST[:, rows], yh[:, 4 * h:4 * h + 4, :], start=True, stop=False)
                        last = nc.tensor.matmul(dst, ST[:, rows], yl[:, 4 * h:4 * h + 4, :], start=False, stop=True)
                    last.then_inc(back_ps, 1)

            def moe_round(r):
                gather(r * (NE + 1))
                with pe.Fori(0, NE) as e:
                    expert(r, e)

            def route():
                pe.wait_ge(rw_l, 1)
                pe.wait_ge(hT_lo_ok, 4 * 6)
                for t in range(NT):
                    rows = slice(t * P, (t + 1) * P)
                    dst = bank[4][:, t * NE:(t + 1) * NE]
                    for k in range(KD):
                        three(dst, hT_hi[:, k, rows], hT_lo[:, k, rows], rw_hi[:, k, :], rw_lo[:, k, :], k == 0, False)
                        last = nc.tensor.matmul(dst, hT_lo[:, k, rows], rw_lo[:, k, :], start=False, stop=k == KD - 1)
                last.then_inc(logit_ps, 1)
                pe.wait_ge(mask_ok, 1)
                tri, ones = cst[:, C_TRI:C_TRI + P], cst[:, C_ONES:C_ONES + P]
                for col, parts in ((0, ((tri, 0),)), (1, ((ones, 0), (tri, 1))), (2, ((ones, 0), (ones, 1)))):
                    for i, (m, t) in enumerate(parts):
                        last = nc.tensor.matmul(bank[5][:, col * NE:(col + 1) * NE], m, mask[:, t, :],
                                                start=i == 0, stop=i == len(parts) - 1)
                last.then_inc(count_ps, 1)

            mixer(0)
            pre_norm(1, 2)
            pe.wait_ge(hT_lo_ok, 4 * 3)
            swiglu(DENSE_AT, DENSE_AT, 0, GD, 3, NT)
            mixer(1)
            pre_norm(3, 5)
            route()
            pe.wait_ge(id_ok, 1)
            pe.wait_ge(xg_l, NT)
            pe.wait_ge(route_ok, 1)
            more = pe.value_load(again[0:1, 0:1], min_val=0, max_val=1)
            moe_round(0)
            with pe.If(more > 0):
                moe_round(1)



def kernel(x, pre_mix_g, post_mix_g, w_in, w_fourier, w_gmlp, w_out, w_spatial, b_spatial,
           gmlp_ln_g, gmlp_ln_b, pre_ffn_g, post_ffn_g, ffn_w1, ffn_w3, ffn_w2,
           router_w, router_b, moe_w1, moe_w3, moe_w2):
    import concourse.bacc as bacc
    from concourse.bass_utils import run_bass_kernel_spmd

    def units(w):
        k, n = w.shape
        return w.reshape(k // 512, 4, P, n // CW, CW).transpose(0, 3, 2, 1, 4).reshape(k // 512, n // CW, P, UNIT)

    def swiglu_units(dst, w1, w3, w2):
        groups = w1.shape[1] // GW
        both = np.empty((groups, 2, P, 4, 2, GW), np.float32)
        for j, w in enumerate((w1, w3)):
            both[:, :, :, :, j, :] = w.reshape(2, 4, P, groups, GW).transpose(3, 0, 2, 1, 4)
        back = w2.reshape(groups, 2, P, D).transpose(0, 2, 1, 3).reshape(groups, P, UNIT)
        at = 0
        for g in range(groups + 2):
            if g < groups:
                dst[at:at + 2] = both[g].reshape(2, P, UNIT)
                at += 2
            if g >= 2:
                dst[at] = back[g - 2]
                at += 1

    a = {n: np.asarray(v) for n, v in dict(w_in=w_in, w_fourier=w_fourier, w_gmlp=w_gmlp, w_out=w_out).items()}
    w1, w3, w2 = (np.asarray(w)[0] for w in (ffn_w1, ffn_w3, ffn_w2))
    e1, e3, e2 = (np.asarray(w)[0] for w in (moe_w1, moe_w3, moe_w2))
    order = (0, 2, 1, 3, 4, 5, 6)
    units_a = np.empty((MOE_AT, P, UNIT), np.float32)
    for l, at in enumerate(MIX_AT):
        w = units(a["w_in"][l])
        for c, src in enumerate(order):
            units_a[at + 2 * c:at + 2 * c + 2] = w[:, src]
        units_a[at + 14:at + 16] = units(a["w_fourier"][l])[0]
        units_a[at + 16:at + 18] = units(a["w_gmlp"][l])[0]
        units_a[at + 18:at + 22] = units(a["w_out"][l]).reshape(4, P, UNIT)
    swiglu_units(units_a[DENSE_AT:DENSE_AT + DENSE_UNITS], w1, w3, w2)
    units_b = np.empty((ROUND_UNITS, P, UNIT), np.float32)
    for e in range(NE):
        swiglu_units(units_b[e * EXPERT_UNITS:(e + 1) * EXPERT_UNITS], e1[e], e3[e], e2[e])

    s = np.arange(SEQ)
    angle = 2 * np.pi * (np.outer(s, s) % SEQ) / SEQ
    seq = np.concatenate([np.cos(angle), np.sin(angle)], axis=1) / np.sqrt(SEQ)
    c = np.arange(P)
    angle = 2 * np.pi * (np.outer(c, c) % P) / P
    consts = np.zeros((P, C_ALL), np.float32)
    consts[:, C_SEQ:C_CH] = seq.reshape(NT, P, 2 * SEQ).transpose(1, 0, 2).reshape(P, -1)
    consts[:, C_CH:C_ID] = np.concatenate([np.cos(angle), -np.sin(angle)], axis=1) / np.sqrt(P)
    consts[:, C_ID:C_IOTA] = np.eye(P)
    consts[:, C_IOTA:C_TRI] = c[None, :]
    consts[:, C_TRI:C_ONES] = c[:, None] <= c[None, :]
    consts[:, C_ONES:C_LOWER] = 1
    consts[:, C_LOWER:C_ALL] = np.tril(np.ones((NE, NE)), -1).reshape(1, -1)

    gains = np.stack([np.asarray(g)[l] for l in range(DEPTH) for g in (pre_mix_g, post_mix_g, pre_ffn_g, post_ffn_g)])
    arrays = {
        "x": np.ascontiguousarray(np.asarray(x).reshape(SEQ, D)),
        "units_a": units_a,
        "units_b": units_b,
        "consts": consts,
        "gains": gains,
        "ln_gb": np.concatenate([np.asarray(gmlp_ln_g), np.asarray(gmlp_ln_b)], axis=1),
        "w_spatial": np.ascontiguousarray(np.asarray(w_spatial).transpose(0, 2, 1, 3)),
        "b_spatial": np.ascontiguousarray(np.asarray(b_spatial).transpose(2, 0, 1)),
        "router_w": np.ascontiguousarray(np.asarray(router_w)[0].reshape(KD, P, NE).transpose(1, 0, 2)),
        "router_b": np.ascontiguousarray(np.asarray(router_b)),
    }
    nc = bacc.Bacc("TRN2", target_bir_lowering=False, num_devices=1)
    ins = [nc.dram_tensor(n, v.shape, mybir.dt.from_np(v.dtype), kind="ExternalInput").ap() for n, v in arrays.items()]
    out = nc.dram_tensor("out", (SEQ, D), F32, kind="ExternalOutput").ap()
    build(nc, *ins, out)
    r = run_bass_kernel_spmd(nc, [arrays], core_ids=[0])
    return r.results[0]["out"].reshape(1, SEQ, D)
```

```python
from contextlib import ExitStack

import numpy as np

import concourse.bass as bass
from concourse import mybir

P = 128
D = 1024
SEQ = 256
NT = SEQ // P
KD = D // P
DEPTH = 2
FW = 512
NG = 4
D_IN = 3 * FW + 2 * D
FF = 2816
NE = 8
FE = 3584
RMS_EPS = 1e-6
LN_EPS = 1e-5

CW = 512
UNIT = 2048
RAW = 6
SPLIT = 3
GW = 256
GD = FF // GW
GE = FE // GW
MIX_UNITS = 2 * (D_IN // CW) + 2 + 2 + 4
DENSE_UNITS = 3 * GD
EXPERT_UNITS = 3 * GE
MIX_AT = (0, MIX_UNITS + DENSE_UNITS)
DENSE_AT = MIX_UNITS
MOE_AT = 2 * MIX_UNITS + DENSE_UNITS
ROUND_UNITS = NE * EXPERT_UNITS
assert EXPERT_UNITS % RAW == 0 and RAW % SPLIT == 0 and ROUND_UNITS % RAW == 0

F32 = mybir.dt.float32
F32R = mybir.dt.float32r
I32 = mybir.dt.int32
ALU = mybir.AluOpType
ACT = mybir.ActivationFunctionType
AX = mybir.AxisListType.X

C_SEQ = 0
C_CH = C_SEQ + NT * 2 * SEQ
C_ID = C_CH + 2 * P
C_IOTA = C_ID + P
C_TRI = C_IOTA + P
C_ONES = C_TRI + P
C_LOWER = C_ONES + P
C_ALL = C_LOWER + NE * NE


def build(nc, x, units_a, units_b, consts, gains, ln_gb, w_spatial, b_spatial, router_w, router_b, out):
    with ExitStack() as ctx:
        def sb(name, shape, dt):
            return ctx.enter_context(nc.sbuf_tensor(name, shape, dt))

        def sem(name):
            return ctx.enter_context(nc.semaphore(name))

        raw = sb("raw", [P, RAW, UNIT], F32)
        w_hi = sb("w_hi", [P, SPLIT, UNIT], F32R)
        w_lo = sb("w_lo", [P, SPLIT, UNIT], F32R)
        x_res = sb("x_res", [P, NT, D], F32)
        xn = sb("xn", [P, NT, D], F32)
        hT_hi = sb("hT_hi", [P, KD, SEQ], F32R)
        hT_lo = sb("hT_lo", [P, KD, SEQ], F32R)
        tok_hi = sb("tok_hi", [P, NT * D], F32R)
        tok_lo = sb("tok_lo", [P, NT * D], F32R)
        gT_hi = sb("gT_hi", [P, 2, 2, SEQ], F32R)
        gT_lo = sb("gT_lo", [P, 2, 2, SEQ], F32R)
        gates = sb("gates", [P, 2, NT, D], F32)
        zbuf = sb("zbuf", [P, 3, NT, FW], F32)
        gain_pre = sb("gain_pre", [P, D], F32)
        gain_post = sb("gain_post", [P, D], F32)
        cst = sb("cst", [P, C_ALL], F32)
        ident_r = sb("ident_r", [P, P], F32R)
        wsT = sb("wsT", [P, NG, P], F32)
        junk = sb("junk", [P, CW], F32)
        ws = sb("ws", [P, NG, P], F32)
        bs = sb("bs", [P, DEPTH, NG], F32)
        rw = sb("rw", [P, KD, NE], F32)
        rw_hi = sb("rw_hi", [P, KD, NE], F32R)
        rw_lo = sb("rw_lo", [P, KD, NE], F32R)
        rb = sb("rb", [P, NE], F32)
        S = sb("S", [P, NT, P], F32R)
        ST = sb("ST", [P, SEQ], F32R)
        sq = sb("sq", [P, 4], F32)
        st = sb("st", [P, 8, NT], F32)
        rstd = sb("rstd", [P, 2, NT], F32)
        bnst = sb("bnst", [P, NT, 6], F32)
        bnag = sb("bnag", [P, NT, 2], F32)
        lg = sb("lg", [P, NT, NE], F32)
        cmp_a = sb("cmp_a", [P, NE, NE], F32)
        cmp_b = sb("cmp_b", [P, NE, NE], F32)
        rank = sb("rank", [P, NT, NE], F32)
        mask = sb("mask", [P, NT, NE], F32)
        gate = sb("gate", [P, NT, NE], F32)
        pos = sb("pos", [P, NT, NE + 1], F32)
        pos2 = sb("pos2", [P, NT, NE + 1], F32)
        rt = sb("rt", [P, 8, NT], F32)
        again = sb("again", [P, 1], I32)

        za, u_act, v_act = zbuf[:, 0], zbuf[:, 1], zbuf[:, 2]
        seqU = xn[:, :, :].rearrange("p t d -> p (t d)").rearrange("p (g n) -> p g n", g=NG)
        faT_hi = tok_hi[:, 0:D].rearrange("p (g s) -> p g s", g=NG)
        faT_lo = tok_lo[:, 0:D].rearrange("p (g s) -> p g s", g=NG)
        sgT_hi = tok_hi[:, D:2 * D].rearrange("p (g s) -> p g s", g=NG)
        sgT_lo = tok_lo[:, D:2 * D].rearrange("p (g s) -> p g s", g=NG)
        silu = zbuf[:, 0].rearrange("p t n -> p (t n)").rearrange("p (b t n) -> p b t n", b=2, t=NT)
        hid = zbuf[:, 1].rearrange("p t n -> p (t n)").rearrange("p (b t n) -> p b t n", b=2, t=NT)
        acc = gates[:, 0]
        tmp = gates[:, 1]
        ident = cst[:, C_ID:C_ID + P]
        iota = cst[:, C_IOTA:C_IOTA + P]
        xg_hi = tok_hi[:, :].rearrange("p (t d) -> p t d", t=NT)
        xg_lo = tok_lo[:, :].rearrange("p (t d) -> p t d", t=NT)
        yh = hT_hi[:, :, P:2 * P]
        yl = hT_lo[:, :, P:2 * P]

        bank = [ctx.enter_context(nc.psum_tensor(f"bank{i}", [P, CW], F32)) for i in range(8)]

        x_loaded = sem("x_loaded")
        cst_loaded = sem("cst_loaded")
        dft_loaded = sem("dft_loaded")
        small_loaded = sem("small_loaded")
        pre_loaded = sem("pre_loaded")
        post_loaded = sem("post_loaded")
        ws_loaded = sem("ws_loaded")
        unit_landed = [sem(f"unit_landed{i}") for i in range(RAW)]
        hi_ready = sem("hi_ready")
        lo_ready = sem("lo_ready")
        unit_used = sem("unit_used")
        sq_done = sem("sq_done")
        x_ready = sem("x_ready")
        tmp_ok = sem("tmp_ok")
        xn_begun = sem("xn_begun")
        xn_ready = sem("xn_ready")
        rstd_ok = sem("rstd_ok")
        out_ps = sem("out_ps")
        hT_ps = sem("hT_ps")
        hT_hi_ok = sem("hT_hi_ok")
        hT_lo_ok = sem("hT_lo_ok")
        z_out = sem("z_out")
        wsT_ps = sem("wsT_ps")
        wsT_ok = sem("wsT_ok")
        fa_ps = sem("fa_ps")
        fa_out = sem("fa_out")
        fb_ps = sem("fb_ps")
        fb_hi = sem("fb_hi")
        fb_lo = sem("fb_lo")
        ln_ok = sem("ln_ok")
        sp_ps = sem("sp_ps")
        sg_ok = sem("sg_ok")
        sgT_ps = sem("sgT_ps")
        sgT_h = sem("sgT_h")
        sgT_l = sem("sgT_l")
        gated = sem("gated")
        merged = sem("merged")
        silu_ok = sem("silu_ok")
        hid_ok = sem("hid_ok")
        gT_ps = sem("gT_ps")
        gT_h = sem("gT_h")
        gT_l = sem("gT_l")
        rw_h = sem("rw_h")
        rw_l = sem("rw_l")
        id_ok = sem("id_ok")
        logit_ps = sem("logit_ps")
        shifted = sem("shifted")
        exp_ok = sem("exp_ok")
        mask_ok = sem("mask_ok")
        count_ps = sem("count_ps")
        xg_h = sem("xg_h")
        xg_l = sem("xg_l")
        route_ok = sem("route_ok")
        S_ok = sem("S_ok")
        pick_ps = sem("pick_ps")
        pick_h = sem("pick_h")
        pick_l = sem("pick_l")
        ST_ps = sem("ST_ps")
        ST_ok = sem("ST_ok")
        y_h = sem("y_h")
        y_l = sem("y_l")
        back_ps = sem("back_ps")
        acc_ok = sem("acc_ok")
        dve_step = sem("dve_step")
        summed = sem("summed")
        stored = sem("stored")

        block = ctx.enter_context(nc.Block())

        def over_groups(eng, groups, peel, step):
            for g in range(peel):
                step(g, g, 0)
            with eng.Fori(0, (groups - peel) // 2) as i:
                for j in range(2):
                    step(i * 2 + (peel + j), peel + j, i)

        Z = (4, 0)

        def quarter(tensor, q):
            return tensor[:, q % 2, (q // 2) * CW:(q // 2 + 1) * CW]

        def hT_quarter(tensor, q):
            return tensor[:, 4 * (q // 2):4 * (q // 2) + 4, (q % 2) * P:(q % 2 + 1) * P]

        def in_four(ap):
            return ap.rearrange("p (k s) -> p k s", k=4)

        def step_unit(g, like):
            return g * 3 - 2 if like >= 2 else g * 2

        @block.sync
        def _(sp):
            for t in range(NT):
                sp.dma_start(x_res[:, t, :], x[t * P:(t + 1) * P, :]).then_inc(x_loaded, 16)
            sp.dma_start(cst[:, C_ID:C_ALL], consts[:, C_ID:C_ALL]).then_inc(cst_loaded, 16)

            def load(u, slot, source):
                sp.dma_start(raw[:, slot, :], source).then_inc(unit_landed[slot], 16)

            for u in range(RAW):
                load(u, u, units_a[u])
                if u == 3:
                    sp.dma_start(cst[:, 0:C_ID], consts[:, 0:C_ID]).then_inc(dft_loaded, 16)
            for first, count, source in ((RAW, MOE_AT - RAW, units_a[RAW:MOE_AT]), (MOE_AT, ROUND_UNITS, units_b)):
                turns = count // RAW
                with sp.Fori(0, turns) as i:
                    for s in range(RAW):
                        sp.wait_ge(lo_ready, i * RAW + (first + s - RAW + 1))
                        load(None, (first + s) % RAW, source[i * RAW + s])
                for s in range(turns * RAW, count):
                    sp.wait_ge(lo_ready, first + s - RAW + 1)
                    load(None, (first + s) % RAW, source[s])
            sp.wait_ge(route_ok, 1)
            more = sp.value_load(again[0:1, 0:1], min_val=0, max_val=1)
            with sp.If(more > 0):
                first = MOE_AT + ROUND_UNITS
                with sp.Fori(0, ROUND_UNITS // RAW) as i:
                    for s in range(RAW):
                        sp.wait_ge(lo_ready, i * RAW + (first + s - RAW + 1))
                        load(None, (first + s) % RAW, units_b[i * RAW + s])
            for q in range(4):
                sp.wait_ge(x_ready, 4 * 3 + q + 1)
                sp.dma_start(out[(q % 2) * P:(q % 2 + 1) * P, (q // 2) * CW:(q // 2 + 1) * CW], quarter(x_res, q))\
                    .then_inc(stored, 16)
            sp.wait_ge(stored, 16 * 4)

        @block.gpsimd
        def _(pool):
            def vector(dst, src, semaphore):
                pool.dma_start(dst, src.partition_broadcast(P)).then_inc(semaphore, 16)

            vector(gain_pre[:, :], gains[0:1, :], pre_loaded)
            pool.dma_start(ws[:, :, :], w_spatial[0]).then_inc(ws_loaded, 16)
            pool.dma_start(bs[:, :, :], b_spatial).then_inc(small_loaded, 16)
            pool.dma_start(rw[:, :, :], router_w).then_inc(small_loaded, 16)
            vector(rb[:, :], router_b, small_loaded)
            vector(gain_post[:, :], gains[1:2, :], post_loaded)
            for l in range(DEPTH):
                pool.wait_ge(xn_ready, 4 * (2 * l + 1))
                vector(gain_pre[:, :], ln_gb[l:l + 1, :], pre_loaded)
                if l == 0:
                    pool.wait_ge(wsT_ps, 1)
                    pool.dma_start(ws[:, :, :], w_spatial[1]).then_inc(ws_loaded, 16)
                pool.wait_ge(ln_ok, NT * (l + 1))
                vector(gain_pre[:, :], gains[4 * l + 2:4 * l + 3, :], pre_loaded)
                pool.wait_ge(x_ready, 4 * (2 * l + 1))
                vector(gain_post[:, :], gains[4 * l + 3:4 * l + 4, :], post_loaded)
                if l == 0:
                    pool.wait_ge(xn_ready, 4 * 2)
                    vector(gain_pre[:, :], gains[4:5, :], pre_loaded)
                    pool.wait_ge(x_ready, 4 * 2)
                    vector(gain_post[:, :], gains[5:6, :], post_loaded)

        @block.scalar
        def _(act):
            def hi(u, like=None, turns=0):
                like = u if like is None else like
                act.wait_ge(unit_landed[like % RAW], turns * 16 + 16 * (like // RAW + 1))
                if not isinstance(u, int) or u >= SPLIT:
                    act.wait_ge(unit_used, u - SPLIT + 1)
                nc.scalar.activation(w_hi[:, like % SPLIT, :], raw[:, like % RAW, :], ACT.Copy).then_inc(hi_ready, 1)

            def square(source, n, q):
                if n or q:
                    act.wait_ge(sq_done, 4 * n + q)
                nc.scalar.activation(junk[:, :], source, ACT.Square, accum_out=sq[:, q:q + 1]).then_inc(sq_done, 1)

            def evict_hT(m, base):
                for q in range(4):
                    act.wait_ge(hT_ps, 4 * m + q + 1)
                    nc.scalar.activation(hT_quarter(hT_hi, q), in_four(bank[base + q][:, :]), ACT.Copy)\
                        .then_inc(hT_hi_ok, 1)

            def pre_norm(n, m, base, ahead=None):
                evict_hT(m, base)
                if ahead is not None:
                    hi(ahead)
                for q in range(4):
                    if n:
                        act.wait_ge(x_ready, 2 * n - 4 + q + 1)
                    square(quarter(x_res, q), n, q)

            def post_norm(n, base, complete):
                for q, (semaphore, value) in enumerate(complete):
                    act.wait_ge(semaphore, value)
                    square(bank[base + q][:, :], n, q)

            def mixer(l):
                at = MIX_AT[l]
                z = Z[l]
                pre_norm(4 * l, 3 * l, z, at + 2)
                for c in range(7):
                    hi(at + 2 * c + 3)
                    if c == 0:
                        act.wait_ge(rstd_ok, 2 * l + 1)
                    act.wait_ge(unit_used, at + 2 * c + 2)
                    for t in range(NT):
                        src = bank[z + 2 * (c % 2) + t][:, :]
                        if c == 0:
                            dst, fn = za[:, t, :], ACT.Copy
                        elif c == 1:
                            dst, fn = v_act[:, t, :], ACT.Gelu
                        elif c == 2:
                            dst, fn = u_act[:, t, :], ACT.Gelu
                        else:
                            h = (c - 3) % 2
                            dst, fn = gates[:, (c - 3) // 2, t, h * CW:(h + 1) * CW], ACT.Sigmoid
                        nc.scalar.activation(dst, src, fn, scale=rstd[:, 0, t:t + 1]).then_inc(z_out, 1)
                    hi(at + 2 * c + 4)
                    if c == 4:
                        for b in range(2):
                            act.wait_ge(fb_ps, 2 * l + b + 1)
                            nc.scalar.activation(faT_hi[:, 2 * b:2 * b + 2, :], bank[(4 - z) + 2 + b][:, :], ACT.Copy)\
                                .then_inc(fb_hi, 1)
                    if c == 6:
                        for b in range(2):
                            act.wait_ge(sgT_ps, 2 * l + b + 1)
                            nc.scalar.activation(sgT_hi[:, 2 * b:2 * b + 2, :], bank[(4 - z) + 2 + b][:, :], ACT.Copy)\
                                .then_inc(sgT_h, 1)
                for u in range(at + 17, at + 20):
                    hi(u)
                for q in range(4):
                    if q == 2:
                        hi(at + 20)
                    act.wait_ge(hT_ps, 4 * (3 * l + 1) + q + 1)
                    nc.scalar.activation(hT_quarter(hT_hi, q), in_four(bank[(4 - z) + q][:, :]), ACT.Copy)\
                        .then_inc(hT_hi_ok, 1)
                for u in range(at + 21, at + 24):
                    hi(u)
                post_norm(4 * l + 1, z, ((out_ps, 5 * l + 1), (unit_used, at + MIX_UNITS - 1),
                                         (out_ps, 5 * l + 2), (unit_used, at + MIX_UNITS)))

            def swiglu(u0, like0, turns0, q0, groups, peel, nt):
                def step(g, like, turns):
                    s, sl = step_unit(g, like), step_unit(like, like)
                    par = like % 2
                    if like or nt == 1:
                        hi(u0 + (s + 2), like0 + sl + 2, turns0 + turns)
                    if like >= 1:
                        act.wait_ge(gT_ps, q0 + g)
                        nc.scalar.activation(gT_hi[:, 1 - par, :, 0:nt * P],
                                             bank[2 + 1 - par][:, 0:2 * nt * P].rearrange("p (f s) -> p f s", f=2),
                                             ACT.Copy).then_inc(gT_h, 1)
                    hi(u0 + (s + 3), like0 + sl + 3, turns0 + turns)
                    if nt == NT and like == 0:
                        act.wait_ge(rstd_ok, 2)
                    act.wait_ge(unit_used, u0 + (s + 2))
                    for t in range(nt):
                        src = bank[t if nt == NT else par][:, 0:GW]
                        scale = rstd[:, 0, t:t + 1] if nt == NT else 1.0
                        nc.scalar.activation(silu[:, par, t, :], src, ACT.Silu, scale=scale).then_inc(silu_ok, NT // nt)
                    if like >= 2:
                        hi(u0 + (s + 4), like0 + sl + 4, turns0 + turns)

                over_groups(act, groups, peel, step)
                par = (groups - 1) % 2
                act.wait_ge(gT_ps, q0 + groups)
                nc.scalar.activation(gT_hi[:, par, :, 0:nt * P],
                                     bank[2 + par][:, 0:2 * nt * P].rearrange("p (f s) -> p f s", f=2),
                                     ACT.Copy).then_inc(gT_h, 1)

            def evict_pick(m):
                act.wait_ge(pick_ps, m + 1)
                for b in range(2):
                    nc.scalar.activation(hT_hi[:, 4 * b:4 * b + 4, 0:P],
                                         bank[6 + b][:, :].rearrange("p (k s) -> p k s", k=4),
                                         ACT.Copy).then_inc(pick_h, 1)

            def expert(r, e, last):
                n = e + NE * r
                act.wait_ge(ST_ps, n + 1)
                nc.scalar.activation(ST[:, :], bank[6][:, 0:SEQ], ACT.Copy).then_inc(ST_ok, 1)
                u0 = n * EXPERT_UNITS + MOE_AT
                swiglu(u0, MOE_AT, n * (EXPERT_UNITS // RAW), n * GE + GD, GE, 4, 1)
                if not last:
                    for i in range(SPLIT - 1):
                        hi(u0 + (EXPERT_UNITS + i), MOE_AT + EXPERT_UNITS + i, n * (EXPERT_UNITS // RAW))
                evict_pick(e + (r * (NE + 1) + 1))
                act.wait_ge(unit_used, u0 + EXPERT_UNITS)
                for h in range(2):
                    nc.scalar.activation(yh[:, 4 * h:4 * h + 4, :],
                                         bank[4 + h][:, :].rearrange("p (k s) -> p k s", k=4),
                                         ACT.Copy).then_inc(y_h, 1)

            def moe_round(r):
                evict_pick(r * (NE + 1))
                with act.Fori(0, NE - 1) as e:
                    expert(r, e, False)
                expert(r, NE - 1, True)

            act.wait_ge(x_loaded, 16 * NT)
            for u in range(SPLIT - 1):
                hi(u)
            mixer(0)
            pre_norm(2, 2, 0, DENSE_AT + 2)
            swiglu(DENSE_AT, DENSE_AT, 0, 0, GD, 3, NT)
            hi(MIX_AT[1])
            hi(MIX_AT[1] + 1)
            act.wait_ge(small_loaded, 48)
            nc.scalar.activation(rw_hi[:, :, :], rw[:, :, :], ACT.Copy).then_inc(rw_h, 1)
            post_norm(3, 4, ((out_ps, 3), (out_ps, 4), (out_ps, 5), (unit_used, DENSE_AT + DENSE_UNITS)))
            mixer(1)
            pre_norm(6, 5, 4)
            act.wait_ge(cst_loaded, 16)
            nc.scalar.activation(ident_r[:, :], ident, ACT.Copy).then_inc(id_ok, 1)
            act.wait_ge(rstd_ok, 4)
            for t in range(NT):
                nc.scalar.activation(xg_hi[:, t, :], xn[:, t, :], ACT.Copy, scale=rstd[:, 0, t:t + 1]).then_inc(xg_h, 1)
            act.wait_ge(shifted, 1)
            nc.scalar.activation(gate[:, :, :], lg[:, :, :], ACT.Exp).then_inc(exp_ok, 1)
            act.wait_ge(route_ok, 1)
            more = act.value_load(again[0:1, 0:1], min_val=0, max_val=1)
            moe_round(0)
            with act.If(more > 0):
                for u in range(SPLIT - 1):
                    hi(MOE_AT + ROUND_UNITS + u)
                moe_round(1)
            act.wait_ge(summed, 1)
            for q in range(4):
                square(quarter(acc, q), 7, q)

        @block.vector
        def _(dve):
            own = [0]

            def link(instruction):
                own[0] += 1
                instruction.then_inc(dve_step, 1)
                dve.wait_ge(dve_step, own[0])

            def lo(u, like=None):
                like = u if like is None else like
                dve.wait_ge(hi_ready, u + 1)
                nc.vector.tensor_tensor(w_lo[:, like % SPLIT, :], raw[:, like % RAW, :],
                                        w_hi[:, like % SPLIT, :].bitcast(F32), ALU.subtract).then_inc(lo_ready, 1)

            def rsqrt(dst, v, part, half, exponent=0):
                nc.vector.tensor_scalar(half, v, -0.5 * 0.25 ** exponent, None, ALU.mult).then_inc(dve_step, 1)
                own[0] += 1
                link(nc.vector.tensor_scalar(part.bitcast(I32), v.bitcast(I32), 1, None, ALU.logical_shift_right))
                link(nc.vector.tensor_scalar(dst.bitcast(I32), part.bitcast(I32), -1.0,
                                             float(0x5F3759DF + (exponent << 23)), ALU.mult, ALU.add))
                for _ in range(3):
                    for t in range(NT):
                        one = slice(t, t + 1)
                        step = nc.vector.tensor_scalar(part[:, one], dst[:, one], dst[:, one], half[:, one],
                                                       ALU.mult, ALU.mult)
                        if t == 0:
                            own[0] += 1
                            step.then_inc(dve_step, 1)
                    link(step)
                    link(nc.vector.scalar_tensor_tensor(dst, part, 1.5, dst, ALU.add, ALU.mult))

            def rms(n, dst):
                dve.wait_ge(sq_done, 4 * (n + 1))
                link(nc.vector.scalar_tensor_tensor(st[:, 1, :], sq[:, 0:2], D * RMS_EPS, sq[:, 2:4],
                                                    ALU.add, ALU.add))
                rsqrt(dst, st[:, 1, :], st[:, 3, :], st[:, 0, :], 5)

            def evict_hT(m, base, q):
                dve.wait_ge(hT_hi_ok, 4 * m + q + 1)
                nc.vector.tensor_tensor(hT_quarter(hT_lo, q), in_four(bank[base + q][:, :]),
                                        hT_quarter(hT_hi, q).bitcast(F32), ALU.subtract).then_inc(hT_lo_ok, 1)

            def scaled(source, q, gain):
                cols = slice((q // 2) * CW, (q // 2 + 1) * CW)
                nc.vector.scalar_tensor_tensor(quarter(tmp, q), source(q), rstd[:, 1, q % 2:q % 2 + 1], gain[:, cols],
                                               ALU.mult, ALU.mult).then_inc(tmp_ok, 1)

            def add(dst, q, count, semaphore):
                dve.wait_ge(tmp_ok, count)
                nc.vector.tensor_tensor(quarter(dst, q), quarter(dst, q), quarter(tmp, q), ALU.add)\
                    .then_inc(semaphore, 1)

            def next_input(load_pre, load_post):
                dve.wait_ge(pre_loaded, 16 * load_pre)
                dve.wait_ge(post_loaded, 16 * load_post)
                for t in range(NT):
                    nc.vector.tensor_tensor(xn[:, t, :], x_res[:, t, :], gain_pre[:, :], ALU.mult)\
                        .then_inc(xn_begun, 1)
                nc.vector.tensor_tensor(gain_pre[:, :], gain_pre[:, :], gain_post[:, :], ALU.mult)\
                    .then_inc(xn_begun, 1)

            def boundary(n, m, old, new, ahead=None):
                out_of = lambda q: bank[old + q][:, :]
                rms(n, rstd[:, 1, :])
                k = n // 2
                dve.wait_ge(xn_begun, 3 * (k + 1))
                scaled(out_of, 0, gain_pre)
                scaled(out_of, 1, gain_pre)
                add(xn, 0, 8 * k + 1, xn_ready)
                add(xn, 1, 8 * k + 2, xn_ready)
                scaled(out_of, 2, gain_pre)
                scaled(out_of, 3, gain_pre)
                evict_hT(m, new, 0)
                evict_hT(m, new, 1)
                add(xn, 2, 8 * k + 3, xn_ready)
                add(xn, 3, 8 * k + 4, xn_ready)
                evict_hT(m, new, 2)
                evict_hT(m, new, 3)
                if ahead is not None:
                    lo(ahead)
                residual(out_of, 8 * k + 4)
                rms(n + 1, rstd[:, 0, :])
                nc.vector.tensor_copy(st[:, 4, :], rstd[:, 0, :]).then_inc(rstd_ok, 1)

            def residual(source, count):
                for q in range(4):
                    scaled(source, q, gain_post)
                    if q:
                        add(x_res, q - 1, count + q, x_ready)
                add(x_res, 3, count + 4, x_ready)

            def spatial_weights(l):
                dve.wait_ge(wsT_ps, l + 1)
                nc.vector.tensor_copy(wsT[:, :, :], in_four(bank[4 - Z[l] + 3][:, :])).then_inc(wsT_ok, 1)

            def mixer(l):
                at = MIX_AT[l]
                z = Z[l]
                side = 4 - z
                for c in range(7):
                    if c == 3:
                        for g in range(NG):
                            dve.wait_ge(fa_ps, NG * l + g + 1)
                            nc.vector.tensor_copy(seqU[:, g, :], bank[side + g][:, :]).then_inc(fa_out, 1)
                    lo(at + 2 * c + 3)
                    if c == 1:
                        spatial_weights(l)
                    if c == 2:
                        dve.wait_ge(z_out, 14 * l + 4)
                        for t in range(NT):
                            link(nc.vector.bn_stats(bnst[:, t, :], v_act[:, t, :]))
                            link(nc.vector.bn_aggr(bnag[:, t, :], bnst[:, t, :]))
                        link(nc.vector.tensor_scalar(st[:, 2, :], bnag[:, :, 1], LN_EPS, None, ALU.add))
                        rsqrt(st[:, 5, :], st[:, 2, :], st[:, 6, :], st[:, 7, :])
                        dve.wait_ge(pre_loaded, 16 * (3 * l + 2))
                        for t in range(NT):
                            link(nc.vector.tensor_scalar(v_act[:, t, :], v_act[:, t, :], bnag[:, t, 0:1],
                                                         st[:, 5, t:t + 1], ALU.subtract, ALU.mult))
                            link(nc.vector.tensor_tensor(v_act[:, t, :], v_act[:, t, :], gain_pre[:, 0:FW], ALU.mult))
                            nc.vector.tensor_tensor(v_act[:, t, :], v_act[:, t, :], gain_pre[:, FW:2 * FW], ALU.add)\
                                .then_inc(ln_ok, 1)
                    if c == 5:
                        for b in range(2):
                            dve.wait_ge(fb_hi, 2 * l + b + 1)
                            nc.vector.tensor_tensor(faT_lo[:, 2 * b:2 * b + 2, :],
                                                    bank[side + 2 + b][:, :].rearrange("p (k s) -> p k s", k=2),
                                                    faT_hi[:, 2 * b:2 * b + 2, :].bitcast(F32), ALU.subtract)\
                                .then_inc(fb_lo, 1)
                    if c == 6:
                        dve.wait_ge(z_out, 14 * l + 6)
                        dve.wait_ge(small_loaded, 48)
                        for t in range(NT):
                            dve.wait_ge(sp_ps, NT * l + t + 1)
                            for g in range(NG):
                                cols = slice(g * P, (g + 1) * P)
                                nc.vector.scalar_tensor_tensor(u_act[:, t, cols], bank[side + t][:, cols],
                                                               bs[:, l, g:g + 1], u_act[:, t, cols],
                                                               ALU.add, ALU.mult).then_inc(sg_ok, 1)
                    lo(at + 2 * c + 4)
                    if c == 5:
                        next_input(3 * l + 3, 2 * l + 1)
                for b in range(2):
                    dve.wait_ge(sgT_h, 2 * l + b + 1)
                    nc.vector.tensor_tensor(sgT_lo[:, 2 * b:2 * b + 2, :],
                                            bank[side + 2 + b][:, :].rearrange("p (k s) -> p k s", k=2),
                                            sgT_hi[:, 2 * b:2 * b + 2, :].bitcast(F32), ALU.subtract)\
                        .then_inc(sgT_l, 1)
                lo(at + 17)
                dve.wait_ge(z_out, 14 * (l + 1))
                for b in range(2):
                    for h in range(2):
                        cols = slice(h * CW, (h + 1) * CW)
                        dve.wait_ge(unit_used, at + 14 + 2 * b + h + 1)
                        for t in range(NT):
                            src = bank[z + 2 * (1 - h) + t] if b == 0 else bank[side + 2 * h + t]
                            nc.vector.tensor_tensor(gates[:, b, t, cols], gates[:, b, t, cols], src[:, :], ALU.mult)\
                                .then_inc(gated, 1)
                        if b:
                            for t in range(NT):
                                dve.wait_ge(gated, 8 * l + 4 + 2 * h + t + 1)
                                nc.vector.tensor_tensor(gates[:, 0, t, cols], gates[:, 0, t, cols],
                                                        gates[:, 1, t, cols], ALU.add).then_inc(merged, 1)
                        if not b or not h:
                            lo(at + 18 + 2 * b + h)
                for q in range(4):
                    evict_hT(3 * l + 1, side, q)
                for u in range(at + 21, at + 24):
                    lo(u)

            def rest(par, nt):
                nc.vector.tensor_tensor(gT_lo[:, par, :, 0:nt * P],
                                        bank[2 + par][:, 0:2 * nt * P].rearrange("p (f s) -> p f s", f=2),
                                        gT_hi[:, par, :, 0:nt * P].bitcast(F32), ALU.subtract).then_inc(gT_l, 1)

            def swiglu(u0, like0, q0, groups, peel, nt):
                def step(g, like, turns):
                    s, sl = step_unit(g, like), step_unit(like, like)
                    par = like % 2
                    if like or nt == 1:
                        lo(u0 + (s + 2), like0 + sl + 2)
                    if like >= 1:
                        dve.wait_ge(gT_h, q0 + g)
                        rest(1 - par, nt)
                    lo(u0 + (s + 3), like0 + sl + 3)
                    dve.wait_ge(silu_ok, (q0 + (g + 1)) * NT)
                    for t in range(nt):
                        src = bank[t if nt == NT else par][:, GW:2 * GW]
                        if nt == NT:
                            ins = nc.vector.scalar_tensor_tensor(hid[:, par, t, :], src, rstd[:, 0, t:t + 1],
                                                                 silu[:, par, t, :], ALU.mult, ALU.mult)
                        else:
                            ins = nc.vector.tensor_tensor(hid[:, par, t, :], src, silu[:, par, t, :], ALU.mult)
                        ins.then_inc(hid_ok, NT // nt)
                    if like >= 2:
                        lo(u0 + (s + 4), like0 + sl + 4)

                over_groups(dve, groups, peel, step)

            def last_rest(q, par, nt):
                dve.wait_ge(gT_h, q)
                rest(par, nt)

            def one_hot(r, e):
                table = (pos, pos2)[r]
                for t in range(NT):
                    nc.vector.tensor_scalar(S[:, t, :], iota, table[:, t, bass.ds(e, 1)], None, ALU.is_equal)\
                        .then_inc(S_ok, 1)

            def evict_pick(m):
                for b in range(2):
                    dve.wait_ge(pick_h, (m * 2) + (b + 1))
                    nc.vector.tensor_tensor(hT_lo[:, 4 * b:4 * b + 4, 0:P],
                                            bank[6 + b][:, :].rearrange("p (k s) -> p k s", k=4),
                                            hT_hi[:, 4 * b:4 * b + 4, 0:P].bitcast(F32), ALU.subtract)\
                        .then_inc(pick_l, 1)

            def expert(r, e, last):
                n = e + NE * r
                u0 = n * EXPERT_UNITS + MOE_AT
                swiglu(u0, MOE_AT, n * GE + GD, GE, 4, 1)
                one_hot(r, e + 1)
                last_rest(n * GE + (GD + GE), (GE - 1) % 2, 1)
                if not last:
                    for i in range(SPLIT - 1):
                        lo(u0 + (EXPERT_UNITS + i), MOE_AT + EXPERT_UNITS + i)
                evict_pick(e + (r * (NE + 1) + 1))
                for h in range(2):
                    dve.wait_ge(y_h, (n * 2) + (h + 1))
                    nc.vector.tensor_tensor(yl[:, 4 * h:4 * h + 4, :],
                                            bank[4 + h][:, :].rearrange("p (k s) -> p k s", k=4),
                                            yh[:, 4 * h:4 * h + 4, :].bitcast(F32), ALU.subtract).then_inc(y_l, 1)
                dve.wait_ge(acc_ok, n * 4 + 1)
                for t in range(NT):
                    dve.wait_ge(back_ps, n * NT + (t + 1))
                    for h in range(2):
                        cols = slice(h * CW, (h + 1) * CW)
                        nc.vector.scalar_tensor_tensor(acc[:, t, cols], bank[2 * t + h][:, :],
                                                       gate[:, t, bass.ds(e, 1)], acc[:, t, cols],
                                                       ALU.mult, ALU.add).then_inc(acc_ok, 1)

            def moe_round(r):
                one_hot(r, 0)
                evict_pick(r * (NE + 1))
                with dve.Fori(0, NE - 1) as e:
                    expert(r, e, False)
                expert(r, NE - 1, True)
                dve.wait_ge(acc_ok, 4 * NE * (r + 1) + 1)

            def route():
                for t in range(NT):
                    dve.wait_ge(xg_h, t + 1)
                    nc.vector.scalar_tensor_tensor(xg_lo[:, t, :], xn[:, t, :], rstd[:, 0, t:t + 1],
                                                   xg_hi[:, t, :].bitcast(F32), ALU.mult, ALU.subtract).then_inc(xg_l, 1)
                nc.vector.memset(acc, 0.0).then_inc(acc_ok, 1)
                dve.wait_ge(logit_ps, 1)
                for t in range(NT):
                    link(nc.vector.scalar_tensor_tensor(lg[:, t, :], bank[4][:, t * NE:(t + 1) * NE], rstd[:, 0, t:t + 1],
                                                        rb[:, :], ALU.mult, ALU.add))
                for t in range(NT):
                    over_e = lg[:, t, :].unsqueeze(1).broadcast_to([P, NE, NE])
                    by_e = lg[:, t, :].unsqueeze(2).broadcast_to([P, NE, NE])
                    link(nc.vector.tensor_tensor(cmp_a[:, :, :], over_e, by_e, ALU.is_gt))
                    link(nc.vector.tensor_tensor(cmp_b[:, :, :], over_e, by_e, ALU.is_equal))
                    link(nc.vector.tensor_tensor(cmp_b[:, :, :], cmp_b[:, :, :],
                                                 cst[:, C_LOWER:C_ALL].rearrange("p (e f) -> p e f", e=NE), ALU.mult))
                    link(nc.vector.tensor_tensor(cmp_a[:, :, :], cmp_a[:, :, :], cmp_b[:, :, :], ALU.add))
                    link(nc.vector.tensor_reduce(rank[:, t, :], cmp_a[:, :, :], AX, ALU.add))
                nc.vector.tensor_scalar(mask[:, :, :], rank[:, :, :], 1.5, None, ALU.is_lt).then_inc(mask_ok, 1)
                link(nc.vector.tensor_reduce(rt[:, 0, :], lg[:, :, :], AX, ALU.max))
                for t in range(NT):
                    link(nc.vector.tensor_scalar(lg[:, t, :], lg[:, t, :], rt[:, 0, t:t + 1], None, ALU.subtract))
                nc.vector.tensor_copy(rt[:, 1, :], rt[:, 0, :]).then_inc(shifted, 1)
                dve.wait_ge(exp_ok, 1)
                dve.wait_ge(mask_ok, 1)
                link(nc.vector.tensor_tensor(gate[:, :, :], gate[:, :, :], mask[:, :, :], ALU.mult))
                link(nc.vector.tensor_reduce(rt[:, 2, :], gate[:, :, :], AX, ALU.add))
                link(nc.vector.reciprocal(rt[:, 3, :], rt[:, 2, :]))
                for t in range(NT):
                    link(nc.vector.tensor_scalar(gate[:, t, :], gate[:, t, :], rt[:, 3, t:t + 1], None, ALU.mult))
                dve.wait_ge(count_ps, 1)
                link(nc.vector.memset(pos[:, :, :], -1.0))
                link(nc.vector.tensor_tensor(pos[:, :, 0:NE],
                                             bank[5][:, 0:NT * NE].rearrange("p (t e) -> p t e", t=NT),
                                             mask[:, :, :], ALU.mult))
                link(nc.vector.tensor_scalar(pos[:, :, 0:NE], pos[:, :, 0:NE], 1.0, None, ALU.subtract))
                link(nc.vector.tensor_scalar(pos2[:, :, :], pos[:, :, :], float(P), None, ALU.subtract))
                link(nc.vector.tensor_reduce(rt[:, 4, 0:1], bank[5][:, NT * NE:(NT + 1) * NE], AX, ALU.max))
                link(nc.vector.tensor_scalar(rt[:, 5, 0:1], rt[:, 4, 0:1], float(P), None, ALU.is_gt))
                nc.vector.tensor_copy(again[:, :], rt[:, 5, 0:1]).then_inc(route_ok, 1)

            dve.wait_ge(x_loaded, 16 * NT)
            dve.wait_ge(pre_loaded, 16)
            for q in range(4):
                cols = slice((q // 2) * CW, (q // 2 + 1) * CW)
                nc.vector.tensor_tensor(quarter(xn, q), quarter(x_res, q), gain_pre[:, cols], ALU.mult)\
                    .then_inc(xn_ready, 1)
            for u in range(SPLIT - 1):
                lo(u)
            for q in range(4):
                evict_hT(0, Z[0], q)
            lo(SPLIT - 1)
            rms(0, rstd[:, 0, :])
            nc.vector.tensor_copy(st[:, 4, :], rstd[:, 0, :]).then_inc(rstd_ok, 1)
            mixer(0)
            boundary(1, 2, Z[0], 0, DENSE_AT + 2)
            swiglu(DENSE_AT, DENSE_AT, 0, GD, 3, NT)
            last_rest(GD, (GD - 1) % 2, NT)
            lo(MIX_AT[1])
            lo(MIX_AT[1] + 1)
            next_input(4, 2)
            dve.wait_ge(rw_h, 1)
            nc.vector.tensor_tensor(rw_lo[:, :, :], rw[:, :, :], rw_hi[:, :, :].bitcast(F32), ALU.subtract)\
                .then_inc(rw_l, 1)
            boundary(3, 3, 4, 0, MIX_AT[1] + 2)
            mixer(1)
            boundary(5, 5, Z[1], 4)
            route()
            dve.wait_ge(route_ok, 1)
            more = dve.value_load(again[0:1, 0:1], min_val=0, max_val=1)
            moe_round(0)
            with dve.If(more > 0):
                for u in range(SPLIT - 1):
                    lo(MOE_AT + ROUND_UNITS + u)
                moe_round(1)
            nc.vector.tensor_copy(rt[:, 6, :], rt[:, 3, :]).then_inc(summed, 1)
            rms(7, rstd[:, 1, :])
            dve.wait_ge(post_loaded, 16 * 4)
            residual(lambda q: quarter(acc, q), 8 * 3)

        @block.tensor
        def _(pe):
            def three(dst, xh, xl, wh, wl, start, stop):
                nc.tensor.matmul(dst, xh, wh, start=start, stop=False)
                nc.tensor.matmul(dst, xh, wl, start=False, stop=False)
                return nc.tensor.matmul(dst, xl, wh, start=False, stop=stop)

            def transposed(tensor, base, q):
                for k in range(4):
                    c0 = (q // 2) * CW + k * P
                    last = nc.tensor.transpose(bank[base + q][:, k * P:(k + 1) * P], tensor[:, q % 2, c0:c0 + P], ident)
                last.then_inc(hT_ps, 1)

            def pre_norm(n, base):
                for q in range(4):
                    pe.wait_ge(xn_ready, 4 * n + q + 1)
                    transposed(xn, base, q)

            def weights(slot, k):
                cols = slice(k * CW, (k + 1) * CW)
                return w_hi[:, slot % SPLIT, cols], w_lo[:, slot % SPLIT, cols]

            def mixer(l):
                at = MIX_AT[l]
                z = Z[l]
                side = 4 - z
                if l == 0:
                    pe.wait_ge(cst_loaded, 16)
                pre_norm(2 * l, z)
                for c in range(7):
                    if c >= 2:
                        pe.wait_ge(z_out, 14 * l + 2 * (c - 1))
                    for h in range(2):
                        u = at + 2 * c + h
                        pe.wait_ge(lo_ready, u + 1)
                        for t in range(NT):
                            if c == 0:
                                pe.wait_ge(hT_lo_ok, 4 * (3 * l) + 2 * h + t + 1)
                            for i in range(4):
                                wh, wl = weights(u, i)
                                rows = slice(t * P, (t + 1) * P)
                                k = 4 * h + i
                                last = three(bank[z + 2 * (c % 2) + t][:, :], hT_hi[:, k, rows], hT_lo[:, k, rows], wh, wl,
                                             k == 0, k == KD - 1)
                        last.then_inc(unit_used, 1)
                    if c == 0:
                        pe.wait_ge(ws_loaded, 16 * (l + 1))
                        if l:
                            pe.wait_ge(x_ready, 4 * 2)
                        for g in range(NG):
                            last = nc.tensor.transpose(bank[side + 3][:, g * P:(g + 1) * P], ws[:, g, :], ident)
                        last.then_inc(wsT_ps, 1)
                    if c == 2:
                        pe.wait_ge(z_out, 14 * l + 2)
                        pe.wait_ge(dft_loaded, 16)
                        pe.wait_ge(wsT_ok, l + 1)
                        for g in range(NG):
                            for t in range(NT):
                                last = nc.tensor.matmul(bank[side + g][:, :], za[:, t, g * P:(g + 1) * P],
                                                        cst[:, C_SEQ + t * 2 * SEQ:C_SEQ + (t + 1) * 2 * SEQ],
                                                        start=t == 0, stop=t == NT - 1)
                            last.then_inc(fa_ps, 1)
                    if c == 3:
                        pe.wait_ge(fa_out, NG * (l + 1))
                        for g in range(NG):
                            dst = bank[side + 2 + g // 2][:, (g % 2) * SEQ:(g % 2 + 1) * SEQ]
                            for i in range(2):
                                last = nc.tensor.matmul(dst, cst[:, C_CH + i * P:C_CH + (i + 1) * P],
                                                        seqU[:, g, i * SEQ:(i + 1) * SEQ], start=i == 0, stop=i == 1)
                            if g % 2:
                                last.then_inc(fb_ps, 1)
                    if c == 4:
                        for t in range(NT):
                            pe.wait_ge(ln_ok, NT * l + t + 1)
                            for g in range(NG):
                                last = nc.tensor.matmul(bank[side + t][:, g * P:(g + 1) * P], wsT[:, g, :],
                                                        v_act[:, t, g * P:(g + 1) * P], start=True, stop=True)
                            last.then_inc(sp_ps, 1)
                pe.wait_ge(fb_lo, 2 * (l + 1))
                pe.wait_ge(sg_ok, NT * NG * (l + 1))
                for g in range(NG):
                    for t in range(NT):
                        c0 = (g % 2) * SEQ + t * P
                        last = nc.tensor.transpose(bank[side + 2 + g // 2][:, c0:c0 + P],
                                                   u_act[:, t, g * P:(g + 1) * P], ident)
                    if g % 2:
                        last.then_inc(sgT_ps, 1)
                for h in range(2):
                    u = at + 14 + h
                    pe.wait_ge(z_out, 14 * l + 12 + 2 * h)
                    pe.wait_ge(lo_ready, u + 1)
                    for t in range(NT):
                        for i in range(4):
                            wh, wl = weights(u, i)
                            rows = slice(t * P, (t + 1) * P)
                            last = three(bank[z + 2 * (1 - h) + t][:, :], faT_hi[:, i, rows], faT_lo[:, i, rows], wh, wl,
                                         i == 0, i == 3)
                    last.then_inc(unit_used, 1)
                pe.wait_ge(sgT_l, 2 * (l + 1))
                for h in range(2):
                    u = at + 16 + h
                    pe.wait_ge(lo_ready, u + 1)
                    for t in range(NT):
                        for i in range(4):
                            wh, wl = weights(u, i)
                            rows = slice(t * P, (t + 1) * P)
                            last = three(bank[side + 2 * h + t][:, :], sgT_hi[:, i, rows], sgT_lo[:, i, rows], wh, wl,
                                         i == 0, i == 3)
                    last.then_inc(unit_used, 1)

                def merge_turn(h):
                    for t in range(NT):
                        pe.wait_ge(merged, 4 * l + 2 * h + t + 1)
                        transposed(gates[:, 0], side, 2 * h + t)

                merge_turn(0)
                for kh in range(2):
                    for h in range(2):
                        u = at + 18 + 2 * kh + h
                        if kh == 0 and h == 1:
                            merge_turn(1)
                        pe.wait_ge(lo_ready, u + 1)
                        for t in range(NT):
                            if h == 0:
                                pe.wait_ge(hT_lo_ok, 4 * (3 * l + 1) + 2 * kh + t + 1)
                            for i in range(4):
                                wh, wl = weights(u, i)
                                rows = slice(t * P, (t + 1) * P)
                                k = 4 * kh + i
                                last = three(bank[z + 2 * h + t][:, :], hT_hi[:, k, rows], hT_lo[:, k, rows], wh, wl,
                                             k == 0, k == KD - 1)
                            if kh and t == 0:
                                last.then_inc(out_ps, 1)
                        last.then_inc(unit_used, 1)

            def swiglu(u0, like0, q0, groups, peel, nt, between=None):
                def up(u, like, h, par):
                    pe.wait_ge(lo_ready, u + 1)
                    for t in range(nt):
                        dst = bank[t if nt == NT else par][:, :]
                        if nt == NT and like == like0 + h:
                            pe.wait_ge(hT_lo_ok, 4 * 2 + 2 * h + t + 1)
                        for i in range(4):
                            wh, wl = weights(like, i)
                            rows = slice(t * P, (t + 1) * P)
                            k = 4 * h + i
                            last = three(dst, hT_hi[:, k, rows], hT_lo[:, k, rows], wh, wl, k == 0, k == KD - 1)
                    last.then_inc(unit_used, 1)

                def turn(par):
                    for f in range(2):
                        for t in range(nt):
                            last = nc.tensor.transpose(bank[2 + par][:, (f * nt + t) * P:(f * nt + t + 1) * P],
                                                       hid[:, par, t, f * P:(f + 1) * P], ident)
                    last.then_inc(gT_ps, 1)

                def down(u, like, q, par, start, stop):
                    pe.wait_ge(gT_l, q + 1)
                    pe.wait_ge(lo_ready, u + 1)
                    if nt == NT and start:
                        pe.wait_ge(x_ready, 4)
                    for h in range(2):
                        for t in range(nt):
                            rows = slice(t * P, (t + 1) * P)
                            for f in range(2):
                                wh, wl = weights(like, 2 * f + h)
                                last = three(bank[4 + h * nt + t][:, :], gT_hi[:, par, f, rows], gT_lo[:, par, f, rows],
                                             wh, wl, start and f == 0, stop and f == 1)
                            if nt == NT and stop and not (h and t):
                                last.then_inc(out_ps, 1)
                    last.then_inc(unit_used, 1)

                def step(g, like, turns):
                    s, sl = step_unit(g, like), step_unit(like, like)
                    par = like % 2
                    back = 1 if nt == NT else 2
                    if like >= back:
                        pe.wait_ge(hid_ok, (q0 + (g + 1 - back)) * NT)
                    up(u0 + s, like0 + sl, 0, par)
                    if like >= 1:
                        pe.wait_ge(hid_ok, (q0 + g) * NT)
                        if like >= 3:
                            pe.wait_ge(gT_l, q0 + (g - 2))
                        turn(1 - par)
                    up(u0 + (s + 1), like0 + sl + 1, 1, par)
                    if like >= 2:
                        down(u0 + (s + 2), like0 + sl + 2, q0 + (g - 2), par, like == 2, False)

                over_groups(pe, groups, peel, step)
                par = (groups - 1) % 2
                down(u0 + (3 * groups - 2), like0 + 3 * groups - 2, q0 + (groups - 2), 1 - par, False, False)
                pe.wait_ge(hid_ok, (q0 + groups) * NT)
                turn(par)
                if between:
                    between()
                down(u0 + (3 * groups - 1), like0 + 3 * groups - 1, q0 + (groups - 1), par, False, True)

            def gather(m):
                pe.wait_ge(S_ok, (m + 1) * NT)
                for b in range(2):
                    for i in range(4):
                        k = 4 * b + i
                        cols = slice(k * P, (k + 1) * P)
                        dst = bank[6 + b][:, i * P:(i + 1) * P]
                        for t in range(NT):
                            nc.tensor.matmul(dst, xg_hi[:, t, cols], S[:, t, :], start=t == 0, stop=False)
                            last = nc.tensor.matmul(dst, xg_lo[:, t, cols], S[:, t, :], start=False, stop=t == NT - 1)
                last.then_inc(pick_ps, 1)

            def expert(r, e):
                n = e + NE * r
                m = e + r * (NE + 1)
                pe.wait_ge(pick_l, (m + 1) * 2)
                for t in range(NT):
                    last = nc.tensor.matmul(bank[6][:, t * P:(t + 1) * P], S[:, t, :], ident_r[:, :],
                                            start=True, stop=True)
                last.then_inc(ST_ps, 1)
                pe.wait_ge(acc_ok, n * 4 + 1)

                def gather_next():
                    pe.wait_ge(ST_ok, n + 1)
                    gather(m + 1)

                swiglu(n * EXPERT_UNITS + MOE_AT, MOE_AT, n * GE + GD, GE, 4, 1, gather_next)
                pe.wait_ge(y_l, (n + 1) * 2)
                for t in range(NT):
                    for h in range(2):
                        dst = bank[2 * t + h][:, :]
                        rows = slice(t * P, (t + 1) * P)
                        nc.tensor.matmul(dst, ST[:, rows], yh[:, 4 * h:4 * h + 4, :], start=True, stop=False)
                        last = nc.tensor.matmul(dst, ST[:, rows], yl[:, 4 * h:4 * h + 4, :], start=False, stop=True)
                    last.then_inc(back_ps, 1)

            def moe_round(r):
                gather(r * (NE + 1))
                with pe.Fori(0, NE) as e:
                    expert(r, e)

            def route():
                pe.wait_ge(rw_l, 1)
                pe.wait_ge(hT_lo_ok, 4 * 6)
                for t in range(NT):
                    rows = slice(t * P, (t + 1) * P)
                    dst = bank[4][:, t * NE:(t + 1) * NE]
                    for k in range(KD):
                        three(dst, hT_hi[:, k, rows], hT_lo[:, k, rows], rw_hi[:, k, :], rw_lo[:, k, :], k == 0, False)
                        last = nc.tensor.matmul(dst, hT_lo[:, k, rows], rw_lo[:, k, :], start=False, stop=k == KD - 1)
                last.then_inc(logit_ps, 1)
                pe.wait_ge(mask_ok, 1)
                tri, ones = cst[:, C_TRI:C_TRI + P], cst[:, C_ONES:C_ONES + P]
                for col, parts in ((0, ((tri, 0),)), (1, ((ones, 0), (tri, 1))), (2, ((ones, 0), (ones, 1)))):
                    for i, (m, t) in enumerate(parts):
                        last = nc.tensor.matmul(bank[5][:, col * NE:(col + 1) * NE], m, mask[:, t, :],
                                                start=i == 0, stop=i == len(parts) - 1)
                last.then_inc(count_ps, 1)

            mixer(0)
            pre_norm(1, 0)
            swiglu(DENSE_AT, DENSE_AT, 0, GD, 3, NT)
            mixer(1)
            pre_norm(3, 4)
            route()
            pe.wait_ge(id_ok, 1)
            pe.wait_ge(xg_l, NT)
            pe.wait_ge(route_ok, 1)
            more = pe.value_load(again[0:1, 0:1], min_val=0, max_val=1)
            moe_round(0)
            with pe.If(more > 0):
                moe_round(1)



def kernel(x, pre_mix_g, post_mix_g, w_in, w_fourier, w_gmlp, w_out, w_spatial, b_spatial,
           gmlp_ln_g, gmlp_ln_b, pre_ffn_g, post_ffn_g, ffn_w1, ffn_w3, ffn_w2,
           router_w, router_b, moe_w1, moe_w3, moe_w2):
    import concourse.bacc as bacc
    from concourse.bass_utils import run_bass_kernel_spmd

    def units(w):
        k, n = w.shape
        return w.reshape(k // 512, 4, P, n // CW, CW).transpose(0, 3, 2, 1, 4).reshape(k // 512, n // CW, P, UNIT)

    def swiglu_units(dst, w1, w3, w2):
        groups = w1.shape[1] // GW
        both = np.empty((groups, 2, P, 4, 2, GW), np.float32)
        for j, w in enumerate((w1, w3)):
            both[:, :, :, :, j, :] = w.reshape(2, 4, P, groups, GW).transpose(3, 0, 2, 1, 4)
        back = w2.reshape(groups, 2, P, D).transpose(0, 2, 1, 3).reshape(groups, P, UNIT)
        at = 0
        for g in range(groups + 2):
            if g < groups:
                dst[at:at + 2] = both[g].reshape(2, P, UNIT)
                at += 2
            if g >= 2:
                dst[at] = back[g - 2]
                at += 1

    a = {n: np.asarray(v) for n, v in dict(w_in=w_in, w_fourier=w_fourier, w_gmlp=w_gmlp, w_out=w_out).items()}
    w1, w3, w2 = (np.asarray(w)[0] for w in (ffn_w1, ffn_w3, ffn_w2))
    e1, e3, e2 = (np.asarray(w)[0] for w in (moe_w1, moe_w3, moe_w2))
    order = (0, 2, 1, 3, 4, 5, 6)
    units_a = np.empty((MOE_AT, P, UNIT), np.float32)
    for l, at in enumerate(MIX_AT):
        w = units(a["w_in"][l])
        for c, src in enumerate(order):
            units_a[at + 2 * c:at + 2 * c + 2] = w[:, src]
        units_a[at + 14:at + 16] = units(a["w_fourier"][l])[0]
        units_a[at + 16:at + 18] = units(a["w_gmlp"][l])[0]
        units_a[at + 18:at + 22] = units(a["w_out"][l]).reshape(4, P, UNIT)
    swiglu_units(units_a[DENSE_AT:DENSE_AT + DENSE_UNITS], w1, w3, w2)
    units_b = np.empty((ROUND_UNITS, P, UNIT), np.float32)
    for e in range(NE):
        swiglu_units(units_b[e * EXPERT_UNITS:(e + 1) * EXPERT_UNITS], e1[e], e3[e], e2[e])

    s = np.arange(SEQ)
    angle = 2 * np.pi * (np.outer(s, s) % SEQ) / SEQ
    seq = np.concatenate([np.cos(angle), np.sin(angle)], axis=1) / np.sqrt(SEQ)
    c = np.arange(P)
    angle = 2 * np.pi * (np.outer(c, c) % P) / P
    consts = np.zeros((P, C_ALL), np.float32)
    consts[:, C_SEQ:C_CH] = seq.reshape(NT, P, 2 * SEQ).transpose(1, 0, 2).reshape(P, -1)
    consts[:, C_CH:C_ID] = np.concatenate([np.cos(angle), -np.sin(angle)], axis=1) / np.sqrt(P)
    consts[:, C_ID:C_IOTA] = np.eye(P)
    consts[:, C_IOTA:C_TRI] = c[None, :]
    consts[:, C_TRI:C_ONES] = c[:, None] <= c[None, :]
    consts[:, C_ONES:C_LOWER] = 1
    consts[:, C_LOWER:C_ALL] = np.tril(np.ones((NE, NE)), -1).reshape(1, -1)

    gains = np.stack([np.asarray(g)[l] for l in range(DEPTH) for g in (pre_mix_g, post_mix_g, pre_ffn_g, post_ffn_g)])
    arrays = {
        "x": np.ascontiguousarray(np.asarray(x).reshape(SEQ, D)),
        "units_a": units_a,
        "units_b": units_b,
        "consts": consts,
        "gains": gains,
        "ln_gb": np.concatenate([np.asarray(gmlp_ln_g), np.asarray(gmlp_ln_b)], axis=1),
        "w_spatial": np.ascontiguousarray(np.asarray(w_spatial).transpose(0, 2, 1, 3)),
        "b_spatial": np.ascontiguousarray(np.asarray(b_spatial).transpose(2, 0, 1)),
        "router_w": np.ascontiguousarray(np.asarray(router_w)[0].reshape(KD, P, NE).transpose(1, 0, 2)),
        "router_b": np.ascontiguousarray(np.asarray(router_b)),
    }
    nc = bacc.Bacc("TRN2", target_bir_lowering=False, num_devices=1)
    ins = [nc.dram_tensor(n, v.shape, mybir.dt.from_np(v.dtype), kind="ExternalInput").ap() for n, v in arrays.items()]
    out = nc.dram_tensor("out", (SEQ, D), F32, kind="ExternalOutput").ap()
    build(nc, *ins, out)
    r = run_bass_kernel_spmd(nc, [arrays], core_ids=[0])
    return r.results[0]["out"].reshape(1, SEQ, D)
```

```python
from contextlib import ExitStack

import numpy as np

import concourse.bass as bass
from concourse import mybir

P = 128
D = 1024
SEQ = 256
NT = SEQ // P
KD = D // P
DEPTH = 2
FW = 512
NG = 4
D_IN = 3 * FW + 2 * D
FF = 2816
NE = 8
FE = 3584
RMS_EPS = 1e-6
LN_EPS = 1e-5

CW = 512
UNIT = 2048
RAW = 6
SPLIT = 3
GW = 256
GD = FF // GW
GE = FE // GW
MIX_UNITS = 2 * (D_IN // CW) + 2 + 2 + 4
DENSE_UNITS = 3 * GD
EXPERT_UNITS = 3 * GE
MIX_AT = (0, MIX_UNITS + DENSE_UNITS)
DENSE_AT = MIX_UNITS
MOE_AT = 2 * MIX_UNITS + DENSE_UNITS
ROUND_UNITS = NE * EXPERT_UNITS
assert EXPERT_UNITS % RAW == 0 and RAW % SPLIT == 0 and ROUND_UNITS % RAW == 0

F32 = mybir.dt.float32
F32R = mybir.dt.float32r
I32 = mybir.dt.int32
ALU = mybir.AluOpType
ACT = mybir.ActivationFunctionType
AX = mybir.AxisListType.X

C_SEQ = 0
C_CH = C_SEQ + NT * 2 * SEQ
C_ID = C_CH + 2 * P
C_IOTA = C_ID + P
C_TRI = C_IOTA + P
C_ONES = C_TRI + P
C_LOWER = C_ONES + P
C_ALL = C_LOWER + NE * NE


def build(nc, x, units_a, units_b, consts, gains, ln_gb, w_spatial, b_spatial, router_w, router_b, out):
    with ExitStack() as ctx:
        def sb(name, shape, dt):
            return ctx.enter_context(nc.sbuf_tensor(name, shape, dt))

        def sem(name):
            return ctx.enter_context(nc.semaphore(name))

        raw = sb("raw", [P, RAW, UNIT], F32)
        w_hi = sb("w_hi", [P, SPLIT, UNIT], F32R)
        w_lo = sb("w_lo", [P, SPLIT, UNIT], F32R)
        x_res = sb("x_res", [P, NT, D], F32)
        xn = sb("xn", [P, NT, D], F32)
        hT_hi = sb("hT_hi", [P, KD, SEQ], F32R)
        hT_lo = sb("hT_lo", [P, KD, SEQ], F32R)
        tok_hi = sb("tok_hi", [P, NT * D], F32R)
        tok_lo = sb("tok_lo", [P, NT * D], F32R)
        gT_hi = sb("gT_hi", [P, 2, 2, SEQ], F32R)
        gT_lo = sb("gT_lo", [P, 2, 2, SEQ], F32R)
        gates = sb("gates", [P, 2, NT, D], F32)
        zbuf = sb("zbuf", [P, 3, NT, FW], F32)
        gain_pre = sb("gain_pre", [P, D], F32)
        gain_post = sb("gain_post", [P, D], F32)
        cst = sb("cst", [P, C_ALL], F32)
        ident_r = sb("ident_r", [P, P], F32R)
        wsT = sb("wsT", [P, NG, P], F32)
        junk = sb("junk", [P, CW], F32)
        ws = sb("ws", [P, NG, P], F32)
        bs = sb("bs", [P, DEPTH, NG], F32)
        rw = sb("rw", [P, KD, NE], F32)
        rw_hi = sb("rw_hi", [P, KD, NE], F32R)
        rw_lo = sb("rw_lo", [P, KD, NE], F32R)
        rb = sb("rb", [P, NE], F32)
        S = sb("S", [P, NT, P], F32R)
        ST = sb("ST", [P, SEQ], F32R)
        sq = sb("sq", [P, 4], F32)
        st = sb("st", [P, 8, NT], F32)
        rstd = sb("rstd", [P, 2, NT], F32)
        bnst = sb("bnst", [P, NT, 6], F32)
        bnag = sb("bnag", [P, NT, 2], F32)
        lg = sb("lg", [P, NT, NE], F32)
        diag = sb("diag", [P, NT, P], F32)
        rank = sb("rank", [P, NT, NE], F32)
        mask = sb("mask", [P, NT, NE], F32)
        gate = sb("gate", [P, NT, NE], F32)
        pos = sb("pos", [P, NT, NE], F32)
        pos2 = sb("pos2", [P, NT, NE], F32)
        rt = sb("rt", [P, 8, NT], F32)
        again = sb("again", [P, 1], I32)

        za, u_act, v_act = zbuf[:, 0], zbuf[:, 1], zbuf[:, 2]
        seqU = xn[:, :, :].rearrange("p t d -> p (t d)").rearrange("p (g n) -> p g n", g=NG)
        faT_hi = tok_hi[:, 0:D].rearrange("p (g s) -> p g s", g=NG)
        faT_lo = tok_lo[:, 0:D].rearrange("p (g s) -> p g s", g=NG)
        sgT_hi = tok_hi[:, D:2 * D].rearrange("p (g s) -> p g s", g=NG)
        sgT_lo = tok_lo[:, D:2 * D].rearrange("p (g s) -> p g s", g=NG)
        silu = zbuf[:, 0].rearrange("p t n -> p (t n)").rearrange("p (b t n) -> p b t n", b=2, t=NT)
        hid = zbuf[:, 1].rearrange("p t n -> p (t n)").rearrange("p (b t n) -> p b t n", b=2, t=NT)
        cmp_a = ws[:, 0, :].rearrange("p (t e f) -> p t e f", t=NT, e=NE)
        cmp_b = ws[:, 1, :].rearrange("p (t e f) -> p t e f", t=NT, e=NE)
        lgT = ws[0:NE, 2:4, :].rearrange("e t s -> e (t s)")
        y_joint = gates[:, 1]
        y_post = gates[:, 0]
        acc = gates[:, 0]
        ident = cst[:, C_ID:C_ID + P]
        iota = cst[:, C_IOTA:C_IOTA + P]
        xg_hi = tok_hi[:, :].rearrange("p (t d) -> p t d", t=NT)
        xg_lo = tok_lo[:, :].rearrange("p (t d) -> p t d", t=NT)
        yh = hT_hi[:, :, P:2 * P]
        yl = hT_lo[:, :, P:2 * P]

        bank = [ctx.enter_context(nc.psum_tensor(f"bank{i}", [P, CW], F32)) for i in range(8)]

        x_loaded = sem("x_loaded")
        cst_loaded = sem("cst_loaded")
        dft_loaded = sem("dft_loaded")
        small_loaded = sem("small_loaded")
        pre_loaded = sem("pre_loaded")
        post_loaded = sem("post_loaded")
        ws_loaded = sem("ws_loaded")
        unit_landed = [sem(f"unit_landed{i}") for i in range(RAW)]
        hi_ready = sem("hi_ready")
        lo_ready = sem("lo_ready")
        unit_used = sem("unit_used")
        sq_done = sem("sq_done")
        x_ready = sem("x_ready")
        xn_begun = sem("xn_begun")
        joint_ok = sem("joint_ok")
        post_ok = sem("post_ok")
        fourth_out = sem("fourth_out")
        fourth_ok = sem("fourth_ok")
        diag_ok = sem("diag_ok")
        y_normed = sem("y_normed")
        xn_ready = sem("xn_ready")
        rstd_ok = sem("rstd_ok")
        out_ps = sem("out_ps")
        hT_ps = sem("hT_ps")
        hT_hi_ok = sem("hT_hi_ok")
        hT_lo_ok = sem("hT_lo_ok")
        z_out = sem("z_out")
        wsT_ps = sem("wsT_ps")
        wsT_ok = sem("wsT_ok")
        fa_ps = sem("fa_ps")
        fa_out = sem("fa_out")
        fb_ps = sem("fb_ps")
        fb_hi = sem("fb_hi")
        fb_lo = sem("fb_lo")
        ln_ok = sem("ln_ok")
        sp_ps = sem("sp_ps")
        sg_ok = sem("sg_ok")
        sgT_ps = sem("sgT_ps")
        sgT_h = sem("sgT_h")
        sgT_l = sem("sgT_l")
        gated = sem("gated")
        merged = sem("merged")
        silu_ok = sem("silu_ok")
        hid_ok = sem("hid_ok")
        gT_ps = sem("gT_ps")
        gT_h = sem("gT_h")
        gT_l = sem("gT_l")
        rw_h = sem("rw_h")
        rw_l = sem("rw_l")
        id_ok = sem("id_ok")
        lgT_ps = sem("lgT_ps")
        lgT_ok = sem("lgT_ok")
        logit_ps = sem("logit_ps")
        shifted = sem("shifted")
        exp_ok = sem("exp_ok")
        mask_ok = sem("mask_ok")
        count_ps = sem("count_ps")
        xg_h = sem("xg_h")
        xg_l = sem("xg_l")
        route_ok = sem("route_ok")
        S_ok = sem("S_ok")
        pick_ps = sem("pick_ps")
        pick_h = sem("pick_h")
        pick_l = sem("pick_l")
        ST_ps = sem("ST_ps")
        ST_ok = sem("ST_ok")
        y_h = sem("y_h")
        y_l = sem("y_l")
        back_ps = sem("back_ps")
        acc_ok = sem("acc_ok")
        dve_step = sem("dve_step")
        last_ok = sem("last_ok")
        stored = sem("stored")

        block = ctx.enter_context(nc.Block())

        def over_groups(eng, groups, peel, step):
            for g in range(peel):
                step(g, g, 0)
            with eng.Fori(0, (groups - peel) // 2) as i:
                for j in range(2):
                    step(i * 2 + (peel + j), peel + j, i)

        Z = (4, 0)
        TOKEN_ORDER = (0, 2, 1, 3)

        def quarter(tensor, q):
            return tensor[:, q % 2, (q // 2) * CW:(q // 2 + 1) * CW]

        def hT_quarter(tensor, q):
            return tensor[:, 4 * (q // 2):4 * (q // 2) + 4, (q % 2) * P:(q % 2 + 1) * P]

        def up_bank(nt, like, t):
            return like % 2 if nt == 1 else 4 + t if like == 1 else t

        def in_four(ap):
            return ap.rearrange("p (k s) -> p k s", k=4)

        def step_unit(g, like):
            return g * 3 - 2 if like >= 2 else g * 2

        @block.sync
        def _(sp):
            def load(slot, source):
                sp.dma_start(raw[:, slot, :], source).then_inc(unit_landed[slot], 16)

            sp.dma_start(cst[:, C_ID:C_ALL], consts[:, C_ID:C_ALL]).then_inc(cst_loaded, 16)
            for u in range(RAW):
                load(u, units_a[u])
                if u == 0:
                    for t in range(NT):
                        sp.dma_start(x_res[:, t, :], x[t * P:(t + 1) * P, :]).then_inc(x_loaded, 16)
                if u == 3:
                    sp.dma_start(cst[:, 0:C_ID], consts[:, 0:C_ID]).then_inc(dft_loaded, 16)
            for first, count, source in ((RAW, MOE_AT - RAW, units_a[RAW:MOE_AT]), (MOE_AT, ROUND_UNITS, units_b)):
                turns = count // RAW
                with sp.Fori(0, turns) as i:
                    for s in range(RAW):
                        sp.wait_ge(lo_ready, i * RAW + (first + s - RAW + 1))
                        load((first + s) % RAW, source[i * RAW + s])
                for s in range(turns * RAW, count):
                    sp.wait_ge(lo_ready, first + s - RAW + 1)
                    load((first + s) % RAW, source[s])
            sp.wait_ge(route_ok, 1)
            more = sp.value_load(again[0:1, 0:1], min_val=0, max_val=1)
            with sp.If(more > 0):
                first = MOE_AT + ROUND_UNITS
                with sp.Fori(0, ROUND_UNITS // RAW) as i:
                    for s in range(RAW):
                        sp.wait_ge(lo_ready, i * RAW + (first + s - RAW + 1))
                        load((first + s) % RAW, units_b[i * RAW + s])
            for q in range(4):
                sp.wait_ge(x_ready, 4 * 3 + q + 1)
                sp.dma_start(out[(q % 2) * P:(q % 2 + 1) * P, (q // 2) * CW:(q // 2 + 1) * CW], quarter(x_res, q))\
                    .then_inc(stored, 16)
            sp.wait_ge(stored, 16 * 4)

        @block.gpsimd
        def _(pool):
            def vector(dst, src, semaphore):
                pool.dma_start(dst, src.partition_broadcast(P)).then_inc(semaphore, 16)

            vector(gain_pre[:, :], gains[0:1, :], pre_loaded)
            pool.dma_start(ws[:, :, :], w_spatial[0]).then_inc(ws_loaded, 16)
            pool.dma_start(bs[:, :, :], b_spatial).then_inc(small_loaded, 16)
            pool.dma_start(rw[:, :, :], router_w).then_inc(small_loaded, 16)
            vector(rb[:, :], router_b, small_loaded)
            vector(gain_post[:, :], gains[1:2, :], post_loaded)
            def fourth(k):
                pool.wait_ge(xn_begun, 3 * (k + 1))
                pool.wait_ge(fourth_out, k + 1)
                nc.gpsimd.tensor_tensor(quarter(y_joint, 3), quarter(y_post, 3), gain_pre[:, CW:D], ALU.mult)\
                    .then_inc(fourth_ok, 1)
                nc.gpsimd.tensor_tensor(quarter(y_post, 3), quarter(y_post, 3), gain_post[:, CW:D], ALU.mult)\
                    .then_inc(fourth_ok, 1)
                pool.wait_ge(fourth_ok, 2 * (k + 1))

            pool.wait_ge(xn_ready, 4)
            vector(gain_pre[:, :], ln_gb[0:1, :], pre_loaded)
            for l in range(DEPTH):
                if l == 0:
                    pool.wait_ge(wsT_ps, 1)
                    pool.dma_start(ws[:, :, :], w_spatial[1]).then_inc(ws_loaded, 16)
                pool.wait_ge(ln_ok, NT * (l + 1))
                vector(gain_pre[:, :], gains[4 * l + 2:4 * l + 3, :], pre_loaded)
                for k in range(2 * l, min(2 * l + 2, 3)):
                    fourth(k)
                    if k < 2:
                        pool.wait_ge(joint_ok, 3 * (k + 1))
                    if k == 0:
                        vector(gain_pre[:, :], gains[4:5, :], pre_loaded)
                    if k == 1:
                        vector(gain_pre[:, :], ln_gb[1:2, :], pre_loaded)
                    pool.wait_ge(post_ok, 3 * (k + 1))
                    vector(gain_post[:, :], gains[2 * k + 3:2 * k + 4, :], post_loaded)
            pool.wait_ge(hT_ps, 4 * 6)
            for i, q in enumerate(TOKEN_ORDER):
                pool.wait_ge(y_normed, i + 1)
                nc.gpsimd.tensor_tensor(quarter(xn, q), quarter(xn, q), zbuf[:, q // 2, q % 2, :], ALU.add)\
                    .then_inc(xn_ready, 1)
            pool.wait_ge(x_ready, 4 * 3)
            nc.gpsimd.memset(acc, 0.0).then_inc(acc_ok, 1)
            pool.wait_ge(route_ok, 1)
            more = pool.value_load(again[0:1, 0:1], min_val=0, max_val=1)
            pool.wait_ge(post_loaded, 16 * 4)
            pool.wait_ge(xg_h, NT)
            for q in range(4):
                pool.wait_ge(acc_ok, more * (4 * NE) + (4 * NE - 2 + q))
                nc.gpsimd.tensor_tensor(quarter(y_joint, q), quarter(acc, q), gain_post[:, (q // 2) * CW:(q // 2 + 1) * CW],
                                        ALU.mult).then_inc(last_ok, 1)

        @block.scalar
        def _(act):
            def hi(u, like=None, turns=0):
                like = u if like is None else like
                act.wait_ge(unit_landed[like % RAW], turns * 16 + 16 * (like // RAW + 1))
                if not isinstance(u, int) or u >= SPLIT:
                    act.wait_ge(unit_used, u - SPLIT + 1)
                nc.scalar.activation(w_hi[:, like % SPLIT, :], raw[:, like % RAW, :], ACT.Copy).then_inc(hi_ready, 1)

            def square(source, n, q):
                if n or q:
                    act.wait_ge(sq_done, 4 * n + q)
                nc.scalar.activation(junk[:, :], source, ACT.Square, accum_out=sq[:, q:q + 1]).then_inc(sq_done, 1)

            def evict_hT(m, base):
                for q in range(4):
                    act.wait_ge(hT_ps, 4 * m + q + 1)
                    nc.scalar.activation(hT_quarter(hT_hi, q), in_four(bank[base + q][:, :]), ACT.Copy)\
                        .then_inc(hT_hi_ok, 1)

            def squares_of_x(n, quarters=range(4)):
                for q in quarters:
                    if n:
                        act.wait_ge(x_ready, 2 * n - 4 + q + 1)
                    square(quarter(x_res, q), n, q)

            def square_out(n, base, q, semaphore, value):
                act.wait_ge(semaphore, value)
                square(bank[base + q][:, :], n, q)
                if q == 3:
                    nc.scalar.activation(quarter(y_post, 3), bank[base + 3][:, :], ACT.Copy).then_inc(fourth_out, 1)

            def mixer(l):
                at = MIX_AT[l]
                z = Z[l]
                for c in range(7):
                    hi(at + 2 * c + 3)
                    if c == 0:
                        act.wait_ge(rstd_ok, 2 * l + 1)
                    act.wait_ge(unit_used, at + 2 * c + 2)
                    for t in range(NT):
                        src = bank[z + 2 * (c % 2) + t][:, :]
                        if c == 0:
                            dst, fn = za[:, t, :], ACT.Copy
                        elif c == 1:
                            dst, fn = v_act[:, t, :], ACT.Gelu
                        elif c == 2:
                            dst, fn = u_act[:, t, :], ACT.Gelu
                        else:
                            h = (c - 3) % 2
                            dst, fn = gates[:, (c - 3) // 2, t, h * CW:(h + 1) * CW], ACT.Sigmoid
                        nc.scalar.activation(dst, src, fn, scale=rstd[:, 0, t:t + 1]).then_inc(z_out, 1)
                    hi(at + 2 * c + 4)
                    if c == 4:
                        for b in range(2):
                            act.wait_ge(fb_ps, 2 * l + b + 1)
                            nc.scalar.activation(faT_hi[:, 2 * b:2 * b + 2, :], bank[(4 - z) + 2 + b][:, :], ACT.Copy)\
                                .then_inc(fb_hi, 1)
                    if c == 6:
                        for b in range(2):
                            act.wait_ge(sgT_ps, 2 * l + b + 1)
                            nc.scalar.activation(sgT_hi[:, 2 * b:2 * b + 2, :], bank[(4 - z) + 2 + b][:, :], ACT.Copy)\
                                .then_inc(sgT_h, 1)
                for u in range(at + 17, at + 20):
                    hi(u)
                for q in range(4):
                    if q == 2:
                        hi(at + 20)
                    act.wait_ge(hT_ps, 4 * (3 * l + 1) + q + 1)
                    nc.scalar.activation(hT_quarter(hT_hi, q), in_four(bank[(4 - z) + q][:, :]), ACT.Copy)\
                        .then_inc(hT_hi_ok, 1)
                hi(at + 21)
                hi(at + 22)
                n = 4 * l + 1
                square_out(n, z, 0, out_ps, 5 * l + 1)
                square_out(n, z, 1, unit_used, at + MIX_UNITS - 1)
                hi(at + 23)
                square_out(n, z, 2, out_ps, 5 * l + 2)
                square_out(n, z, 3, unit_used, at + MIX_UNITS)

            def swiglu(u0, like0, turns0, q0, groups, peel, nt, n_expert=None):
                def step(g, like, turns):
                    s, sl = step_unit(g, like), step_unit(like, like)
                    par = like % 2
                    if like:
                        hi(u0 + (s + 2), like0 + sl + 2, turns0 + turns)
                    if like >= 1:
                        act.wait_ge(gT_ps, q0 + g)
                        nc.scalar.activation(gT_hi[:, 1 - par, :, 0:nt * P],
                                             bank[2 + 1 - par][:, 0:2 * nt * P].rearrange("p (f s) -> p f s", f=2),
                                             ACT.Copy).then_inc(gT_h, 1)
                    hi(u0 + (s + 3), like0 + sl + 3, turns0 + turns)
                    if nt == 1 and like == 0:
                        act.wait_ge(ST_ps, n_expert + 1)
                        nc.scalar.activation(ST[:, :], bank[6][:, 0:SEQ], ACT.Copy).then_inc(ST_ok, 1)
                    if nt == NT and like == 0:
                        act.wait_ge(rstd_ok, 2)
                    act.wait_ge(unit_used, u0 + (s + 2))
                    for t in range(nt):
                        src = bank[up_bank(nt, like, t)][:, 0:GW]
                        scale = rstd[:, 0, t:t + 1] if nt == NT else 1.0
                        nc.scalar.activation(silu[:, par, t, :], src, ACT.Silu, scale=scale).then_inc(silu_ok, NT // nt)
                    if like >= 2:
                        hi(u0 + (s + 4), like0 + sl + 4, turns0 + turns)

                over_groups(act, groups, peel, step)
                par = (groups - 1) % 2
                act.wait_ge(gT_ps, q0 + groups)
                nc.scalar.activation(gT_hi[:, par, :, 0:nt * P],
                                     bank[2 + par][:, 0:2 * nt * P].rearrange("p (f s) -> p f s", f=2),
                                     ACT.Copy).then_inc(gT_h, 1)

            def evict_pick(m):
                for b in range(2):
                    act.wait_ge(pick_ps, (m * 2) + (b + 1))
                    nc.scalar.activation(hT_hi[:, 4 * b:4 * b + 4, 0:P], in_four(bank[6 + b][:, :]), ACT.Copy)\
                        .then_inc(pick_h, 1)

            def expert(r, e, last):
                n = e + NE * r
                u0 = n * EXPERT_UNITS + MOE_AT
                swiglu(u0, MOE_AT, n * (EXPERT_UNITS // RAW), n * GE + GD, GE, 4, 1, n)
                if not last:
                    for i in range(SPLIT - 1):
                        hi(u0 + (EXPERT_UNITS + i), MOE_AT + EXPERT_UNITS + i, n * (EXPERT_UNITS // RAW))
                    evict_pick(n + 1)
                for h in range(2):
                    if h == 0:
                        act.wait_ge(out_ps, n + (7 + 1))
                    else:
                        act.wait_ge(unit_used, u0 + EXPERT_UNITS)
                    nc.scalar.activation(yh[:, 4 * h:4 * h + 4, :], in_four(bank[4 + h][:, :]), ACT.Copy)\
                        .then_inc(y_h, 1)
                if not last:
                    i = SPLIT - 1
                    hi(u0 + (EXPERT_UNITS + i), MOE_AT + EXPERT_UNITS + i, n * (EXPERT_UNITS // RAW))

            def moe_round(r):
                if r:
                    evict_pick(NE * r)
                with act.Fori(0, NE - 1) as e:
                    expert(r, e, False)
                expert(r, NE - 1, True)

            hi(0)
            act.wait_ge(x_loaded, 16 * NT)
            squares_of_x(0, (0, 1))
            evict_hT(0, Z[0])
            squares_of_x(0, (2, 3))
            for u in range(1, SPLIT):
                hi(u)
            act.wait_ge(cst_loaded, 16)
            nc.scalar.activation(ident_r[:, :], ident, ACT.Copy).then_inc(id_ok, 1)
            mixer(0)
            evict_hT(2, 0)
            hi(DENSE_AT + 2)
            squares_of_x(2)
            swiglu(DENSE_AT, DENSE_AT, 0, 0, GD, 3, NT)
            hi(MIX_AT[1])
            hi(MIX_AT[1] + 1)
            for q in range(3):
                square_out(3, 4, q, out_ps, 3 + q)
            square_out(3, 4, 3, unit_used, DENSE_AT + DENSE_UNITS)
            evict_hT(3, 0)
            hi(MIX_AT[1] + 2)
            squares_of_x(4)
            act.wait_ge(small_loaded, 48)
            nc.scalar.activation(rw_hi[:, :, :], rw[:, :, :], ACT.Copy).then_inc(rw_h, 1)
            mixer(1)
            act.wait_ge(diag_ok, NT * 3)
            act.wait_ge(joint_ok, 3 * 3)
            for q in TOKEN_ORDER:
                if q == 3:
                    act.wait_ge(fourth_ok, 2 * 2 + 1)
                nc.scalar.activation(zbuf[:, q // 2, q % 2, :], quarter(y_joint, q), ACT.Copy,
                                     scale=rstd[:, 1, q % 2:q % 2 + 1]).then_inc(y_normed, 1)
            evict_hT(5, 4)
            squares_of_x(6)
            hi(MOE_AT + 2)
            act.wait_ge(lgT_ps, 1)
            nc.scalar.activation(lgT[:, :], bank[4][0:NE, 0:SEQ], ACT.Copy).then_inc(lgT_ok, 1)
            act.wait_ge(rstd_ok, 4)
            for t in range(NT):
                act.wait_ge(xn_ready, 4 + 2 * (t + 1))
                nc.scalar.activation(xg_hi[:, t, :], xn[:, t, :], ACT.Copy, scale=rstd[:, 0, t:t + 1]).then_inc(xg_h, 1)
            act.wait_ge(shifted, 1)
            nc.scalar.activation(gate[:, :, :], lg[:, :, :], ACT.Exp).then_inc(exp_ok, 1)
            evict_pick(0)
            moe_round(0)
            act.wait_ge(route_ok, 1)
            more = act.value_load(again[0:1, 0:1], min_val=0, max_val=1)
            with act.If(more > 0):
                for u in range(SPLIT):
                    hi(MOE_AT + ROUND_UNITS + u)
                moe_round(1)
            for q in range(4):
                act.wait_ge(acc_ok, more * (4 * NE) + (4 * NE - 2 + q))
                square(quarter(acc, q), 7, q)

        @block.vector
        def _(dve):
            own = [0]

            def link(instruction):
                own[0] += 1
                instruction.then_inc(dve_step, 1)
                dve.wait_ge(dve_step, own[0])

            def lo(u, like=None):
                like = u if like is None else like
                dve.wait_ge(hi_ready, u + 1)
                nc.vector.tensor_tensor(w_lo[:, like % SPLIT, :], raw[:, like % RAW, :],
                                        w_hi[:, like % SPLIT, :].bitcast(F32), ALU.subtract).then_inc(lo_ready, 1)

            def rsqrt(dst, v, part, half, exponent=0):
                nc.vector.tensor_scalar(half, v, -0.5 * 0.25 ** exponent, None, ALU.mult).then_inc(dve_step, 1)
                own[0] += 1
                link(nc.vector.tensor_scalar(part.bitcast(I32), v.bitcast(I32), 1, None, ALU.logical_shift_right))
                link(nc.vector.tensor_scalar(dst.bitcast(I32), part.bitcast(I32), -1.0,
                                             float(0x5F3759DF + (exponent << 23)), ALU.mult, ALU.add))
                for _ in range(3):
                    for t in range(NT):
                        one = slice(t, t + 1)
                        step = nc.vector.tensor_scalar(part[:, one], dst[:, one], dst[:, one], half[:, one],
                                                       ALU.mult, ALU.mult)
                        if t == 0:
                            own[0] += 1
                            step.then_inc(dve_step, 1)
                    link(step)
                    link(nc.vector.scalar_tensor_tensor(dst, part, 1.5, dst, ALU.add, ALU.mult))

            def rms(n, dst):
                dve.wait_ge(sq_done, 4 * (n + 1))
                link(nc.vector.scalar_tensor_tensor(st[:, 1, :], sq[:, 0:2], D * RMS_EPS, sq[:, 2:4],
                                                    ALU.add, ALU.add))
                rsqrt(dst, st[:, 1, :], st[:, 3, :], st[:, 0, :], 5)

            def evict_hT(m, base, q):
                dve.wait_ge(hT_hi_ok, 4 * m + q + 1)
                nc.vector.tensor_tensor(hT_quarter(hT_lo, q), in_four(bank[base + q][:, :]),
                                        hT_quarter(hT_hi, q).bitcast(F32), ALU.subtract).then_inc(hT_lo_ok, 1)

            def next_input(load_pre, load_post):
                dve.wait_ge(pre_loaded, 16 * load_pre)
                dve.wait_ge(post_loaded, 16 * load_post)
                for t in range(NT):
                    nc.vector.tensor_tensor(xn[:, t, :], x_res[:, t, :], gain_pre[:, :], ALU.mult)\
                        .then_inc(xn_begun, 1)
                nc.vector.tensor_tensor(gain_pre[:, :], gain_pre[:, :], gain_post[:, :], ALU.mult)\
                    .then_inc(xn_begun, 1)

            def times_joint(n, q, old):
                if q == 0:
                    dve.wait_ge(xn_begun, 3 * (n // 2 + 1))
                dve.wait_ge(sq_done, 4 * n + q + 1)
                nc.vector.tensor_tensor(quarter(y_joint, q), bank[old + q][:, :],
                                        gain_pre[:, (q // 2) * CW:(q // 2 + 1) * CW], ALU.mult).then_inc(joint_ok, 1)

            def times_post(n, q, old):
                dve.wait_ge(sq_done, 4 * n + q + 1)
                nc.vector.tensor_tensor(quarter(y_post, q), bank[old + q][:, :],
                                        gain_post[:, (q // 2) * CW:(q // 2 + 1) * CW], ALU.mult).then_inc(post_ok, 1)

            def residual(source, q):
                nc.vector.scalar_tensor_tensor(quarter(x_res, q), quarter(source, q), rstd[:, 1, q % 2:q % 2 + 1],
                                               quarter(x_res, q), ALU.mult, ALU.add).then_inc(x_ready, 1)

            def boundary(n, m, old, new, posted, ahead=None):
                k = n // 2

                def take(q):
                    if q < 3:
                        dve.wait_ge(post_ok, 3 * k + q + 1)
                    else:
                        dve.wait_ge(fourth_ok, 2 * (k + 1))
                    residual(y_post, q)

                rms(n, rstd[:, 1, :])
                for t in range(NT):
                    nc.vector.tensor_scalar(diag[:, t, :], ident, rstd[:, 1, t:t + 1], None, ALU.mult)\
                        .then_inc(diag_ok, 1)
                for q in range(posted, 3):
                    times_post(n, q, old)
                urgent = n == 5
                if urgent:
                    take(0)
                    take(1)
                evict_hT(m, new, 0)
                evict_hT(m, new, 1)
                if urgent:
                    take(2)
                    take(3)
                else:
                    take(0)
                evict_hT(m, new, 2)
                evict_hT(m, new, 3)
                if not urgent:
                    for q in range(1, 4):
                        take(q)
                if ahead is not None:
                    lo(ahead)
                rms(n + 1, rstd[:, 0, :])
                nc.vector.tensor_copy(st[:, 4, :], rstd[:, 0, :]).then_inc(rstd_ok, 1)

            def spatial_weights(l):
                dve.wait_ge(wsT_ps, l + 1)
                nc.vector.tensor_copy(wsT[:, :, :], in_four(bank[4 - Z[l] + 3][:, :])).then_inc(wsT_ok, 1)

            def mixer(l):
                at = MIX_AT[l]
                z = Z[l]
                side = 4 - z
                for c in range(7):
                    if c == 3:
                        for g in range(NG):
                            dve.wait_ge(fa_ps, NG * l + g + 1)
                            nc.vector.tensor_copy(seqU[:, g, :], bank[side + g][:, :]).then_inc(fa_out, 1)
                    lo(at + 2 * c + 3)
                    if c == 1:
                        spatial_weights(l)
                    if c == 2:
                        dve.wait_ge(z_out, 14 * l + 4)
                        for t in range(NT):
                            link(nc.vector.bn_stats(bnst[:, t, :], v_act[:, t, :]))
                            link(nc.vector.bn_aggr(bnag[:, t, :], bnst[:, t, :]))
                        link(nc.vector.tensor_scalar(st[:, 2, :], bnag[:, :, 1], LN_EPS, None, ALU.add))
                        rsqrt(st[:, 5, :], st[:, 2, :], st[:, 6, :], st[:, 7, :])
                        dve.wait_ge(pre_loaded, 16 * (3 * l + 2))
                        for t in range(NT):
                            link(nc.vector.tensor_scalar(v_act[:, t, :], v_act[:, t, :], bnag[:, t, 0:1],
                                                         st[:, 5, t:t + 1], ALU.subtract, ALU.mult))
                            link(nc.vector.tensor_tensor(v_act[:, t, :], v_act[:, t, :], gain_pre[:, 0:FW], ALU.mult))
                            nc.vector.tensor_tensor(v_act[:, t, :], v_act[:, t, :], gain_pre[:, FW:2 * FW], ALU.add)\
                                .then_inc(ln_ok, 1)
                    if c == 5:
                        for b in range(2):
                            dve.wait_ge(fb_hi, 2 * l + b + 1)
                            nc.vector.tensor_tensor(faT_lo[:, 2 * b:2 * b + 2, :],
                                                    bank[side + 2 + b][:, :].rearrange("p (k s) -> p k s", k=2),
                                                    faT_hi[:, 2 * b:2 * b + 2, :].bitcast(F32), ALU.subtract)\
                                .then_inc(fb_lo, 1)
                    if c == 6:
                        dve.wait_ge(z_out, 14 * l + 6)
                        dve.wait_ge(small_loaded, 48)
                        for t in range(NT):
                            dve.wait_ge(sp_ps, NT * l + t + 1)
                            for g in range(NG):
                                cols = slice(g * P, (g + 1) * P)
                                nc.vector.scalar_tensor_tensor(u_act[:, t, cols], bank[side + t][:, cols],
                                                               bs[:, l, g:g + 1], u_act[:, t, cols],
                                                               ALU.add, ALU.mult).then_inc(sg_ok, 1)
                    lo(at + 2 * c + 4)
                    if c == 5:
                        next_input(3 * l + 3, 2 * l + 1)
                for b in range(2):
                    dve.wait_ge(sgT_h, 2 * l + b + 1)
                    nc.vector.tensor_tensor(sgT_lo[:, 2 * b:2 * b + 2, :],
                                            bank[side + 2 + b][:, :].rearrange("p (k s) -> p k s", k=2),
                                            sgT_hi[:, 2 * b:2 * b + 2, :].bitcast(F32), ALU.subtract)\
                        .then_inc(sgT_l, 1)
                lo(at + 17)
                dve.wait_ge(z_out, 14 * (l + 1))

                def gate_branch(b, h):
                    dve.wait_ge(unit_used, at + 14 + 2 * b + h + 1)
                    cols = slice(h * CW, (h + 1) * CW)
                    for t in range(NT):
                        src = bank[z + 2 * (1 - h) + t] if b == 0 else bank[side + 2 * h + t]
                        nc.vector.tensor_tensor(gates[:, b, t, cols], gates[:, b, t, cols], src[:, :], ALU.mult)\
                            .then_inc(gated, 1)

                def merge(h):
                    cols = slice(h * CW, (h + 1) * CW)
                    for t in range(NT):
                        dve.wait_ge(gated, 8 * l + 4 + 2 * h + t + 1)
                        nc.vector.tensor_tensor(gates[:, 0, t, cols], gates[:, 0, t, cols],
                                                gates[:, 1, t, cols], ALU.add).then_inc(merged, 1)

                gate_branch(0, 0)
                lo(at + 18)
                gate_branch(0, 1)
                gate_branch(1, 0)
                merge(0)
                evict_hT(3 * l + 1, side, 0)
                evict_hT(3 * l + 1, side, 1)
                lo(at + 19)
                gate_branch(1, 1)
                merge(1)
                lo(at + 20)
                evict_hT(3 * l + 1, side, 2)
                evict_hT(3 * l + 1, side, 3)
                lo(at + 21)
                lo(at + 22)
                n = 4 * l + 1
                for q in range(2):
                    times_joint(n, q, z)
                    times_post(n, q, z)
                lo(at + 23)
                times_joint(n, 2, z)

            def rest(par, nt):
                nc.vector.tensor_tensor(gT_lo[:, par, :, 0:nt * P],
                                        bank[2 + par][:, 0:2 * nt * P].rearrange("p (f s) -> p f s", f=2),
                                        gT_hi[:, par, :, 0:nt * P].bitcast(F32), ALU.subtract).then_inc(gT_l, 1)

            def swiglu(u0, like0, q0, groups, peel, nt):
                def step(g, like, turns):
                    s, sl = step_unit(g, like), step_unit(like, like)
                    par = like % 2
                    if like:
                        lo(u0 + (s + 2), like0 + sl + 2)
                    if like >= 1:
                        dve.wait_ge(gT_h, q0 + g)
                        rest(1 - par, nt)
                    lo(u0 + (s + 3), like0 + sl + 3)
                    dve.wait_ge(silu_ok, (q0 + (g + 1)) * NT)
                    for t in range(nt):
                        src = bank[up_bank(nt, like, t)][:, GW:2 * GW]
                        if nt == NT:
                            ins = nc.vector.scalar_tensor_tensor(hid[:, par, t, :], src, rstd[:, 0, t:t + 1],
                                                                 silu[:, par, t, :], ALU.mult, ALU.mult)
                        else:
                            ins = nc.vector.tensor_tensor(hid[:, par, t, :], src, silu[:, par, t, :], ALU.mult)
                        ins.then_inc(hid_ok, NT // nt)
                    if like >= 2:
                        lo(u0 + (s + 4), like0 + sl + 4)

                over_groups(dve, groups, peel, step)

            def last_rest(q, par, nt):
                dve.wait_ge(gT_h, q)
                rest(par, nt)

            def one_hot(r, e):
                table = (pos, pos2)[r]
                for t in range(NT):
                    nc.vector.tensor_scalar(S[:, t, :], iota, table[:, t, bass.ds(e, 1)], None, ALU.is_equal)\
                        .then_inc(S_ok, 1)

            def evict_pick(m):
                for b in range(2):
                    dve.wait_ge(pick_h, (m * 2) + (b + 1))
                    nc.vector.tensor_tensor(hT_lo[:, 4 * b:4 * b + 4, 0:P],
                                            bank[6 + b][:, :].rearrange("p (k s) -> p k s", k=4),
                                            hT_hi[:, 4 * b:4 * b + 4, 0:P].bitcast(F32), ALU.subtract)\
                        .then_inc(pick_l, 1)

            def expert(r, e, last):
                n = e + NE * r
                u0 = n * EXPERT_UNITS + MOE_AT
                swiglu(u0, MOE_AT, n * GE + GD, GE, 4, 1)
                if not last:
                    one_hot(r, e + 1)
                last_rest(n * GE + (GD + GE), (GE - 1) % 2, 1)
                if not last:
                    for i in range(SPLIT - 1):
                        lo(u0 + (EXPERT_UNITS + i), MOE_AT + EXPERT_UNITS + i)
                    evict_pick(n + 1)
                for h in range(2):
                    dve.wait_ge(y_h, (n * 2) + (h + 1))
                    nc.vector.tensor_tensor(yl[:, 4 * h:4 * h + 4, :],
                                            bank[4 + h][:, :].rearrange("p (k s) -> p k s", k=4),
                                            yh[:, 4 * h:4 * h + 4, :].bitcast(F32), ALU.subtract).then_inc(y_l, 1)
                dve.wait_ge(acc_ok, n * 4 + 1)
                for q in range(4):
                    dve.wait_ge(back_ps, n * 4 + (q + 1))
                    nc.vector.scalar_tensor_tensor(quarter(acc, q), bank[q][:, :], gate[:, q % 2, bass.ds(e, 1)],
                                                   quarter(acc, q), ALU.mult, ALU.add).then_inc(acc_ok, 1)
                if not last:
                    i = SPLIT - 1
                    lo(u0 + (EXPERT_UNITS + i), MOE_AT + EXPERT_UNITS + i)

            def moe_round(r):
                if r:
                    one_hot(r, 0)
                    evict_pick(NE)
                with dve.Fori(0, NE - 1) as e:
                    expert(r, e, False)
                expert(r, NE - 1, True)
                dve.wait_ge(acc_ok, 4 * NE * (r + 1) + 1)

            def route():
                dve.wait_ge(logit_ps, 1)
                for t in range(NT):
                    ins = nc.vector.scalar_tensor_tensor(lg[:, t, :], bank[5][:, t * NE:(t + 1) * NE],
                                                         rstd[:, 0, t:t + 1], rb[:, :], ALU.mult, ALU.add)
                    if t == 0:
                        own[0] += 1
                        ins.then_inc(dve_step, 1)
                link(ins)
                over_e = lg[:, :, :].unsqueeze(2).broadcast_to([P, NT, NE, NE])
                by_e = lg[:, :, :].unsqueeze(3).broadcast_to([P, NT, NE, NE])
                lower = cst[:, C_LOWER:C_ALL].rearrange("p (e f) -> p e f", e=NE).unsqueeze(1)\
                    .broadcast_to([P, NT, NE, NE])
                own[0] += 1
                nc.vector.tensor_tensor(cmp_a, over_e, by_e, ALU.is_gt).then_inc(dve_step, 1)
                link(nc.vector.tensor_tensor(cmp_b, over_e, by_e, ALU.is_equal))
                link(nc.vector.tensor_tensor(cmp_b, cmp_b, lower, ALU.mult))
                link(nc.vector.tensor_tensor(cmp_a, cmp_a, cmp_b, ALU.add))
                link(nc.vector.tensor_reduce(rank[:, :, :], cmp_a, AX, ALU.add))
                nc.vector.tensor_scalar(mask[:, :, :], rank[:, :, :], 1.5, None, ALU.is_lt).then_inc(mask_ok, 1)
                for t in range(NT):
                    dve.wait_ge(xg_h, t + 1)
                    nc.vector.scalar_tensor_tensor(xg_lo[:, t, :], xn[:, t, :], rstd[:, 0, t:t + 1],
                                                   xg_hi[:, t, :].bitcast(F32), ALU.mult, ALU.subtract).then_inc(xg_l, 1)
                dve.wait_ge(count_ps, 1)
                dve.wait_ge(mask_ok, 1)
                link(nc.vector.tensor_tensor(pos[:, :, :],
                                             bank[4][:, 0:NT * NE].rearrange("p (t e) -> p t e", t=NT),
                                             mask[:, :, :], ALU.mult))
                one_hot(0, 0)
                link(nc.vector.tensor_reduce(rt[:, 0, :], lg[:, :, :], AX, ALU.max))
                for t in range(NT):
                    link(nc.vector.tensor_scalar(lg[:, t, :], lg[:, t, :], rt[:, 0, t:t + 1], None, ALU.subtract))
                nc.vector.tensor_copy(rt[:, 1, :], rt[:, 0, :]).then_inc(shifted, 1)
                link(nc.vector.tensor_scalar(pos2[:, :, :], pos[:, :, :], float(P), None, ALU.subtract))
                link(nc.vector.tensor_reduce(rt[:, 4, 0:1], bank[4][:, NT * NE:(NT + 1) * NE], AX, ALU.max))
                link(nc.vector.tensor_scalar(rt[:, 5, 0:1], rt[:, 4, 0:1], float(P), None, ALU.is_gt))
                nc.vector.tensor_copy(again[:, :], rt[:, 5, 0:1]).then_inc(route_ok, 1)
                lo(MOE_AT + 2)
                evict_pick(0)
                dve.wait_ge(exp_ok, 1)
                link(nc.vector.tensor_tensor(gate[:, :, :], gate[:, :, :], mask[:, :, :], ALU.mult))
                link(nc.vector.tensor_reduce(rt[:, 2, :], gate[:, :, :], AX, ALU.add))
                link(nc.vector.reciprocal(rt[:, 3, :], rt[:, 2, :]))
                for t in range(NT):
                    link(nc.vector.tensor_scalar(gate[:, t, :], gate[:, t, :], rt[:, 3, t:t + 1], None, ALU.mult))

            lo(0)
            dve.wait_ge(x_loaded, 16 * NT)
            dve.wait_ge(pre_loaded, 16)
            for q in range(4):
                cols = slice((q // 2) * CW, (q // 2 + 1) * CW)
                nc.vector.tensor_tensor(quarter(xn, q), quarter(x_res, q), gain_pre[:, cols], ALU.mult)\
                    .then_inc(xn_ready, 1)
            for q in range(4):
                evict_hT(0, Z[0], q)
            for u in range(1, SPLIT - 1):
                lo(u)
            rms(0, rstd[:, 0, :])
            nc.vector.tensor_copy(st[:, 4, :], rstd[:, 0, :]).then_inc(rstd_ok, 1)
            lo(SPLIT - 1)
            mixer(0)
            boundary(1, 2, Z[0], 0, 2, DENSE_AT + 2)
            swiglu(DENSE_AT, DENSE_AT, 0, GD, 3, NT)
            next_input(4, 2)
            last_rest(GD, (GD - 1) % 2, NT)
            lo(MIX_AT[1])
            lo(MIX_AT[1] + 1)
            for q in range(3):
                times_joint(3, q, 4)
            boundary(3, 3, 4, 0, 0, MIX_AT[1] + 2)
            dve.wait_ge(rw_h, 1)
            nc.vector.tensor_tensor(rw_lo[:, :, :], rw[:, :, :], rw_hi[:, :, :].bitcast(F32), ALU.subtract)\
                .then_inc(rw_l, 1)
            mixer(1)
            boundary(5, 5, Z[1], 4, 2)
            route()
            dve.wait_ge(route_ok, 1)
            more = dve.value_load(again[0:1, 0:1], min_val=0, max_val=1)
            moe_round(0)
            with dve.If(more > 0):
                for u in range(SPLIT):
                    lo(MOE_AT + ROUND_UNITS + u)
                moe_round(1)
            rms(7, rstd[:, 1, :])
            for q in range(4):
                dve.wait_ge(last_ok, q + 1)
                residual(y_joint, q)

        @block.tensor
        def _(pe):
            def three(dst, xh, xl, wh, wl, start, stop):
                nc.tensor.matmul(dst, xh, wh, start=start, stop=False)
                nc.tensor.matmul(dst, xh, wl, start=False, stop=False)
                return nc.tensor.matmul(dst, xl, wh, start=False, stop=stop)

            def transposed(tensor, base, q):
                for k in range(4):
                    c0 = (q // 2) * CW + k * P
                    last = nc.tensor.transpose(bank[base + q][:, k * P:(k + 1) * P], tensor[:, q % 2, c0:c0 + P], ident)
                last.then_inc(hT_ps, 1)

            def next_hT(k, base):
                pe.wait_ge(id_ok, 1)
                pe.wait_ge(xn_begun, 3 * k + 2)
                for q in range(4):
                    nc.tensor.matmul(bank[base + q][:, :], ident_r[0:1, :], ident_r[0:1, 1:2].broadcast_to([1, CW]),
                                     start=True, stop=False)
                    for i in range(4):
                        c0 = (q // 2) * CW + i * P
                        nc.tensor.matmul(bank[base + q][:, i * P:(i + 1) * P], xn[:, q % 2, c0:c0 + P], ident,
                                         start=False, stop=False)
                pe.wait_ge(diag_ok, NT * (k + 1))
                pe.wait_ge(joint_ok, 3 * (k + 1))
                for q in range(4):
                    if q == 3:
                        pe.wait_ge(fourth_ok, 2 * k + 1)
                    for i in range(4):
                        c0 = (q // 2) * CW + i * P
                        last = nc.tensor.matmul(bank[base + q][:, i * P:(i + 1) * P], y_joint[:, q % 2, c0:c0 + P],
                                                diag[:, q % 2, :], start=False, stop=i == 3)
                    last.then_inc(hT_ps, 1)

            def keep_warm(spare, count):
                for _ in range(count):
                    nc.tensor.matmul(spare[:, 0:P], ident, ident, start=True, stop=True)

            def weights(slot, k):
                cols = slice(k * CW, (k + 1) * CW)
                return w_hi[:, slot % SPLIT, cols], w_lo[:, slot % SPLIT, cols]

            def mixer(l):
                at = MIX_AT[l]
                z = Z[l]
                side = 4 - z
                for c in range(7):
                    if c >= 2:
                        pe.wait_ge(z_out, 14 * l + 2 * (c - 1))
                    for h in range(2):
                        u = at + 2 * c + h
                        pe.wait_ge(lo_ready, u + 1)
                        for t in range(NT):
                            if c == 0:
                                pe.wait_ge(hT_lo_ok, 4 * (3 * l) + 2 * h + t + 1)
                            for i in range(4):
                                wh, wl = weights(u, i)
                                rows = slice(t * P, (t + 1) * P)
                                k = 4 * h + i
                                last = three(bank[z + 2 * (c % 2) + t][:, :], hT_hi[:, k, rows], hT_lo[:, k, rows], wh, wl,
                                             k == 0, k == KD - 1)
                        last.then_inc(unit_used, 1)
                    if c == 0:
                        pe.wait_ge(ws_loaded, 16 * (l + 1))
                        if l:
                            pe.wait_ge(x_ready, 4 * 2)
                        for g in range(NG):
                            last = nc.tensor.transpose(bank[side + 3][:, g * P:(g + 1) * P], ws[:, g, :], ident)
                        last.then_inc(wsT_ps, 1)
                    if c == 2:
                        pe.wait_ge(z_out, 14 * l + 2)
                        pe.wait_ge(dft_loaded, 16)
                        pe.wait_ge(wsT_ok, l + 1)
                        for g in range(NG):
                            for t in range(NT):
                                last = nc.tensor.matmul(bank[side + g][:, :], za[:, t, g * P:(g + 1) * P],
                                                        cst[:, C_SEQ + t * 2 * SEQ:C_SEQ + (t + 1) * 2 * SEQ],
                                                        start=t == 0, stop=t == NT - 1)
                            last.then_inc(fa_ps, 1)
                    if c == 3:
                        pe.wait_ge(fa_out, NG * (l + 1))
                        for g in range(NG):
                            dst = bank[side + 2 + g // 2][:, (g % 2) * SEQ:(g % 2 + 1) * SEQ]
                            for i in range(2):
                                last = nc.tensor.matmul(dst, cst[:, C_CH + i * P:C_CH + (i + 1) * P],
                                                        seqU[:, g, i * SEQ:(i + 1) * SEQ], start=i == 0, stop=i == 1)
                            if g % 2:
                                last.then_inc(fb_ps, 1)
                    if c == 4:
                        for t in range(NT):
                            pe.wait_ge(ln_ok, NT * l + t + 1)
                            for g in range(NG):
                                last = nc.tensor.matmul(bank[side + t][:, g * P:(g + 1) * P], wsT[:, g, :],
                                                        v_act[:, t, g * P:(g + 1) * P], start=True, stop=True)
                            last.then_inc(sp_ps, 1)
                def branch(u, xh, xl, base, t):
                    for i in range(4):
                        wh, wl = weights(u, i)
                        rows = slice(t * P, (t + 1) * P)
                        last = three(bank[base + t][:, :], xh[:, i, rows], xl[:, i, rows], wh, wl, i == 0, i == 3)
                    return last

                def fourier_half(h):
                    u = at + 14 + h
                    pe.wait_ge(z_out, 14 * l + 12 + 2 * h)
                    pe.wait_ge(lo_ready, u + 1)
                    for t in range(NT):
                        last = branch(u, faT_hi, faT_lo, z + 2 * (1 - h), t)
                    last.then_inc(unit_used, 1)

                def merge_turn(h):
                    for t in range(NT):
                        pe.wait_ge(merged, 4 * l + 2 * h + t + 1)
                        transposed(gates[:, 0], side, 2 * h + t)

                pe.wait_ge(fb_lo, 2 * (l + 1))
                fourier_half(0)
                pe.wait_ge(sg_ok, NT * NG * (l + 1))
                for g in range(NG):
                    for t in range(NT):
                        c0 = (g % 2) * SEQ + t * P
                        last = nc.tensor.transpose(bank[side + 2 + g // 2][:, c0:c0 + P],
                                                   u_act[:, t, g * P:(g + 1) * P], ident)
                    if g % 2:
                        last.then_inc(sgT_ps, 1)
                fourier_half(1)
                pe.wait_ge(sgT_l, 2 * (l + 1))
                for h in range(2):
                    u = at + 16 + h
                    pe.wait_ge(lo_ready, u + 1)
                    branch(u, sgT_hi, sgT_lo, side + 2 * h, 0)
                    if h:
                        merge_turn(0)
                    branch(u, sgT_hi, sgT_lo, side + 2 * h, 1).then_inc(unit_used, 1)
                for kh in range(2):
                    for h in range(2):
                        u = at + 18 + 2 * kh + h
                        if kh == 0 and h == 1:
                            merge_turn(1)
                        pe.wait_ge(lo_ready, u + 1)
                        for t in range(NT):
                            if h == 0:
                                pe.wait_ge(hT_lo_ok, 4 * (3 * l + 1) + 2 * kh + t + 1)
                            for i in range(4):
                                wh, wl = weights(u, i)
                                rows = slice(t * P, (t + 1) * P)
                                k = 4 * kh + i
                                last = three(bank[z + 2 * h + t][:, :], hT_hi[:, k, rows], hT_lo[:, k, rows], wh, wl,
                                             k == 0, k == KD - 1)
                            if kh and t == 0:
                                last.then_inc(out_ps, 1)
                        last.then_inc(unit_used, 1)

            def swiglu(u0, like0, q0, groups, peel, nt, input_half, begun=None, between=None):
                def up(u, like, h, rank):
                    pe.wait_ge(lo_ready, u + 1)
                    for t in range(nt):
                        dst = bank[up_bank(nt, rank, t)][:, :]
                        if rank == 0:
                            input_half(h, t)
                        for i in range(4):
                            wh, wl = weights(like, i)
                            rows = slice(t * P, (t + 1) * P)
                            k = 4 * h + i
                            last = three(dst, hT_hi[:, k, rows], hT_lo[:, k, rows], wh, wl, k == 0, k == KD - 1)
                    last.then_inc(unit_used, 1)

                def turn(par):
                    for f in range(2):
                        for t in range(nt):
                            last = nc.tensor.transpose(bank[2 + par][:, (f * nt + t) * P:(f * nt + t + 1) * P],
                                                       hid[:, par, t, f * P:(f + 1) * P], ident)
                    last.then_inc(gT_ps, 1)

                def down(u, like, q, par, start, stop, middle=None):
                    pe.wait_ge(gT_l, q + 1)
                    pe.wait_ge(lo_ready, u + 1)
                    for h in range(2):
                        if h and middle:
                            middle()
                        for t in range(nt):
                            rows = slice(t * P, (t + 1) * P)
                            for f in range(2):
                                wh, wl = weights(like, 2 * f + h)
                                last = three(bank[4 + h * nt + t][:, :], gT_hi[:, par, f, rows], gT_lo[:, par, f, rows],
                                             wh, wl, start and f == 0, stop and f == 1)
                            if stop and not (h and t == nt - 1):
                                last.then_inc(out_ps, 1)
                    last.then_inc(unit_used, 1)

                def step(g, like, turns):
                    s, sl = step_unit(g, like), step_unit(like, like)
                    par = like % 2
                    if nt == NT and like == 1:
                        pe.wait_ge(x_ready, 4)
                    elif like >= 2:
                        pe.wait_ge(hid_ok, (q0 + (g - 1 if nt == 1 or like == 2 else g)) * NT)
                    up(u0 + s, like0 + sl, 0, like)
                    if like >= 1:
                        pe.wait_ge(hid_ok, (q0 + g) * NT)
                        if like >= 3:
                            pe.wait_ge(gT_l, q0 + (g - 2))
                        turn(1 - par)
                    up(u0 + (s + 1), like0 + sl + 1, 1, like)
                    if like == 0 and begun:
                        begun()
                    if like >= 2:
                        down(u0 + (s + 2), like0 + sl + 2, q0 + (g - 2), par, like == 2, False)

                over_groups(pe, groups, peel, step)
                par = (groups - 1) % 2

                def last_turn():
                    pe.wait_ge(hid_ok, (q0 + groups) * NT)
                    turn(par)

                down(u0 + (3 * groups - 2), like0 + 3 * groups - 2, q0 + (groups - 2), 1 - par, False, False, last_turn)
                if between:
                    between()
                down(u0 + (3 * groups - 1), like0 + 3 * groups - 1, q0 + (groups - 1), par, False, True)

            def gather(m):
                pe.wait_ge(S_ok, (m + 1) * NT)
                for b in range(2):
                    for i in range(4):
                        k = 4 * b + i
                        cols = slice(k * P, (k + 1) * P)
                        dst = bank[6 + b][:, i * P:(i + 1) * P]
                        for t in range(NT):
                            nc.tensor.matmul(dst, xg_hi[:, t, cols], S[:, t, :], start=t == 0, stop=False)
                            last = nc.tensor.matmul(dst, xg_lo[:, t, cols], S[:, t, :], start=False, stop=t == NT - 1)
                    last.then_inc(pick_ps, 1)

            def expert(r, e, last):
                n = e + NE * r
                pe.wait_ge(acc_ok, n * 4 + 1)

                def input_half(h, t):
                    pe.wait_ge(pick_l, (n * 2) + (h + 1))

                def turn_S():
                    for t in range(NT):
                        ins = nc.tensor.matmul(bank[6][:, t * P:(t + 1) * P], S[:, t, :], ident_r[:, :],
                                               start=True, stop=True)
                    ins.then_inc(ST_ps, 1)

                def gather_next():
                    pe.wait_ge(ST_ok, n + 1)
                    gather(n + 1)

                swiglu(n * EXPERT_UNITS + MOE_AT, MOE_AT, n * GE + GD, GE, 4, 1, input_half, turn_S,
                       None if last else gather_next)
                if last:
                    pe.wait_ge(ST_ok, n + 1)
                for q in range(4):
                    t, h = q % 2, q // 2
                    pe.wait_ge(y_l, (n * 2) + (h + 1))
                    rows = slice(t * P, (t + 1) * P)
                    nc.tensor.matmul(bank[q][:, :], ST[:, rows], yh[:, 4 * h:4 * h + 4, :], start=True, stop=False)
                    nc.tensor.matmul(bank[q][:, :], ST[:, rows], yl[:, 4 * h:4 * h + 4, :], start=False, stop=True)\
                        .then_inc(back_ps, 1)

            def moe_round(r):
                gather(NE * r)
                with pe.Fori(0, NE - 1) as e:
                    expert(r, e, False)
                expert(r, NE - 1, True)

            def route():
                pe.wait_ge(rw_l, 1)
                dst = bank[4][0:NE, 0:SEQ]
                for k in range(KD):
                    if k % 4 == 0:
                        pe.wait_ge(hT_lo_ok, 4 * 5 + k // 2 + 2)
                    for a, w in enumerate((rw_hi, rw_lo)):
                        for b, h in enumerate((hT_hi, hT_lo)):
                            last = nc.tensor.matmul(dst, w[:, k, :], h[:, k, :], start=k == 0 and a + b == 0,
                                                    stop=k == KD - 1 and a + b == 2)
                last.then_inc(lgT_ps, 1)
                pe.wait_ge(lgT_ok, 1)
                for t in range(NT):
                    last = nc.tensor.transpose(bank[5][:, t * NE:(t + 1) * NE], lgT[:, t * P:(t + 1) * P],
                                               cst[0:NE, C_ID:C_ID + NE])
                last.then_inc(logit_ps, 1)
                keep_warm(bank[7], 12)
                pe.wait_ge(mask_ok, 1)
                tri, ones = cst[:, C_TRI:C_TRI + P], cst[:, C_ONES:C_ONES + P]
                for col, parts in ((0, ((tri, 0),)), (1, ((ones, 0), (tri, 1))), (2, ((ones, 0), (ones, 1)))):
                    for i, (m, t) in enumerate(parts):
                        last = nc.tensor.matmul(bank[4][:, col * NE:(col + 1) * NE], m, mask[:, t, :],
                                                start=i == 0, stop=i == len(parts) - 1)
                last.then_inc(count_ps, 1)

            pe.wait_ge(cst_loaded, 16)
            keep_warm(bank[0], 24)
            for q in range(4):
                pe.wait_ge(xn_ready, q + 1)
                transposed(xn, Z[0], q)
            mixer(0)
            next_hT(0, 0)
            swiglu(DENSE_AT, DENSE_AT, 0, GD, 3, NT, lambda h, t: pe.wait_ge(hT_lo_ok, 4 * 2 + 2 * h + t + 1))
            next_hT(1, 0)
            mixer(1)
            next_hT(2, 4)
            route()
            keep_warm(bank[7], 11)
            pe.wait_ge(xg_l, NT)
            moe_round(0)
            pe.wait_ge(route_ok, 1)
            more = pe.value_load(again[0:1, 0:1], min_val=0, max_val=1)
            with pe.If(more > 0):
                moe_round(1)


def kernel(x, pre_mix_g, post_mix_g, w_in, w_fourier, w_gmlp, w_out, w_spatial, b_spatial,
           gmlp_ln_g, gmlp_ln_b, pre_ffn_g, post_ffn_g, ffn_w1, ffn_w3, ffn_w2,
           router_w, router_b, moe_w1, moe_w3, moe_w2):
    import concourse.bacc as bacc
    from concourse.bass_utils import run_bass_kernel_spmd

    def units(w):
        k, n = w.shape
        return w.reshape(k // 512, 4, P, n // CW, CW).transpose(0, 3, 2, 1, 4).reshape(k // 512, n // CW, P, UNIT)

    def swiglu_units(dst, w1, w3, w2):
        groups = w1.shape[1] // GW
        both = np.empty((groups, 2, P, 4, 2, GW), np.float32)
        for j, w in enumerate((w1, w3)):
            both[:, :, :, :, j, :] = w.reshape(2, 4, P, groups, GW).transpose(3, 0, 2, 1, 4)
        back = w2.reshape(groups, 2, P, D).transpose(0, 2, 1, 3).reshape(groups, P, UNIT)
        at = 0
        for g in range(groups + 2):
            if g < groups:
                dst[at:at + 2] = both[g].reshape(2, P, UNIT)
                at += 2
            if g >= 2:
                dst[at] = back[g - 2]
                at += 1

    a = {n: np.asarray(v) for n, v in dict(w_in=w_in, w_fourier=w_fourier, w_gmlp=w_gmlp, w_out=w_out).items()}
    w1, w3, w2 = (np.asarray(w)[0] for w in (ffn_w1, ffn_w3, ffn_w2))
    e1, e3, e2 = (np.asarray(w)[0] for w in (moe_w1, moe_w3, moe_w2))
    order = (0, 2, 1, 3, 4, 5, 6)
    units_a = np.empty((MOE_AT, P, UNIT), np.float32)
    for l, at in enumerate(MIX_AT):
        w = units(a["w_in"][l])
        for c, src in enumerate(order):
            units_a[at + 2 * c:at + 2 * c + 2] = w[:, src]
        units_a[at + 14:at + 16] = units(a["w_fourier"][l])[0]
        units_a[at + 16:at + 18] = units(a["w_gmlp"][l])[0]
        units_a[at + 18:at + 22] = units(a["w_out"][l]).reshape(4, P, UNIT)
    swiglu_units(units_a[DENSE_AT:DENSE_AT + DENSE_UNITS], w1, w3, w2)
    units_b = np.empty((ROUND_UNITS, P, UNIT), np.float32)
    for e in range(NE):
        swiglu_units(units_b[e * EXPERT_UNITS:(e + 1) * EXPERT_UNITS], e1[e], e3[e], e2[e])

    s = np.arange(SEQ)
    angle = 2 * np.pi * (np.outer(s, s) % SEQ) / SEQ
    seq = np.concatenate([np.cos(angle), np.sin(angle)], axis=1) / np.sqrt(SEQ)
    c = np.arange(P)
    angle = 2 * np.pi * (np.outer(c, c) % P) / P
    consts = np.zeros((P, C_ALL), np.float32)
    consts[:, C_SEQ:C_CH] = seq.reshape(NT, P, 2 * SEQ).transpose(1, 0, 2).reshape(P, -1)
    consts[:, C_CH:C_ID] = np.concatenate([np.cos(angle), -np.sin(angle)], axis=1) / np.sqrt(P)
    consts[:, C_ID:C_IOTA] = np.eye(P)
    consts[:, C_IOTA:C_TRI] = 1 + c[None, :]
    consts[:, C_TRI:C_ONES] = c[:, None] <= c[None, :]
    consts[:, C_ONES:C_LOWER] = 1
    consts[:, C_LOWER:C_ALL] = np.tril(np.ones((NE, NE)), -1).reshape(1, -1)

    gains = np.stack([np.asarray(g)[l] for l in range(DEPTH) for g in (pre_mix_g, post_mix_g, pre_ffn_g, post_ffn_g)])
    arrays = {
        "x": np.ascontiguousarray(np.asarray(x).reshape(SEQ, D)),
        "units_a": units_a,
        "units_b": units_b,
        "consts": consts,
        "gains": gains,
        "ln_gb": np.concatenate([np.asarray(gmlp_ln_g), np.asarray(gmlp_ln_b)], axis=1),
        "w_spatial": np.ascontiguousarray(np.asarray(w_spatial).transpose(0, 2, 1, 3)),
        "b_spatial": np.ascontiguousarray(np.asarray(b_spatial).transpose(2, 0, 1)),
        "router_w": np.ascontiguousarray(np.asarray(router_w)[0].reshape(KD, P, NE).transpose(1, 0, 2)),
        "router_b": np.ascontiguousarray(np.asarray(router_b)),
    }
    nc = bacc.Bacc("TRN2", target_bir_lowering=False, num_devices=1)
    ins = [nc.dram_tensor(n, v.shape, mybir.dt.from_np(v.dtype), kind="ExternalInput").ap() for n, v in arrays.items()]
    out = nc.dram_tensor("out", (SEQ, D), F32, kind="ExternalOutput").ap()
    build(nc, *ins, out)
    r = run_bass_kernel_spmd(nc, [arrays], core_ids=[0])
    return r.results[0]["out"].reshape(1, SEQ, D)
```
